# Optimizing a Trainium2 kernel written in Bass

```python
import math
import jax
import jax.numpy as jnp
from jax import lax
import numpy as np

D_MODEL = 1024
BATCH = 1
SEQ = 256
DEPTH = 1

HEAD_DIM = 64
DIL_GROUPS = ((128, 1), (512, 4), (2048, 16))
N_DIL_GROUPS = 3
DIL_HEADS = 4
MOBA_HEADS = 8
MOBA_BLOCK = 256
MOBA_TOPK = 3
MOBA_Q_CHUNK = 16
N_SELF_HEADS = N_DIL_GROUPS * DIL_HEADS + MOBA_HEADS
REL_BUCKETS = 32
REL_MAX_DIST = 2048
N_MEM = 256
CROSS_HEADS = 4
CROSS_HEAD_DIM = 128
PEER_HEADS = 8
PEER_N_KEYS = 128
PEER_N_EXPERTS = PEER_N_KEYS * PEER_N_KEYS
PEER_KEY_DIM = 256
PEER_TOPK = 16
PEER_TOKEN_CHUNK = 128
RMS_EPS = 1e-6
NEG_INF = -1e30
DIL_WIDTH = N_DIL_GROUPS * 3 * DIL_HEADS * HEAD_DIM
MOBA_WIDTH = 3 * MOBA_HEADS * HEAD_DIM
GATE_WIDTH = 2 * D_MODEL
IN_COLS = DIL_WIDTH + MOBA_WIDTH + GATE_WIDTH

kernel_name = 'hybrid_dilated_moba_peer_layer'

def rmsnorm(x, g):
    xf = x.astype(jnp.float32)
    y = xf * lax.rsqrt(jnp.mean(xf * xf, axis=-1, keepdims=True) + RMS_EPS)
    return (y * g.astype(jnp.float32)).astype(x.dtype)

def t5_bucket(n):
    max_exact = REL_BUCKETS // 2
    nf = jnp.maximum(n, 1).astype(jnp.float32)
    large = max_exact + (jnp.log(nf / max_exact) / math.log(REL_MAX_DIST / max_exact)
                         * (REL_BUCKETS - max_exact)).astype(jnp.int32)
    large = jnp.minimum(large, REL_BUCKETS - 1)
    return jnp.where(n < max_exact, n, large)

def dilated_group(q, k, v, window, dilation, bias_tab):
    B, S, H, hd = q.shape
    d = dilation
    blk = window // d
    L = S // d
    nb = -(-L // blk)
    Lp = nb * blk

    def to_sub(t):
        return t.reshape(B, L, d, H, hd).transpose(0, 2, 3, 1, 4)

    qs = jnp.pad(to_sub(q), ((0, 0), (0, 0), (0, 0), (0, Lp - L), (0, 0))).reshape(B, d, H, nb, blk, hd)

    def windows(t):
        tp = jnp.pad(to_sub(t), ((0, 0), (0, 0), (0, 0), (blk, Lp - L), (0, 0))).reshape(B, d, H, nb + 1, blk, hd)
        return jnp.concatenate([tp[:, :, :, :-1], tp[:, :, :, 1:]], axis=-2)

    kw = windows(k)
    vw = windows(v)
    logits = jnp.einsum('bdhnqc,bdhnkc->bdhnqk', qs, kw).astype(jnp.float32) * (hd ** -0.5)
    rel = (blk + jnp.arange(blk))[:, None] - jnp.arange(2 * blk)[None, :]
    in_window = (rel >= 0) & (rel <= blk)
    key_sub = (jnp.arange(nb)[:, None] - 1) * blk + jnp.arange(2 * blk)[None, :]
    mask = in_window[None] & (key_sub >= 0)[:, None, :]
    bias = bias_tab[t5_bucket(jnp.clip(rel, 0) * d)].transpose(2, 0, 1).astype(jnp.float32)
    logits = jnp.where(mask, logits + bias[:, None], NEG_INF)
    lse = jax.nn.logsumexp(logits, axis=-1)
    p = jnp.exp(logits - lse[..., None])
    out = jnp.einsum('bdhnqk,bdhnkc->bdhnqc', p, vw.astype(jnp.float32))
    out = out.reshape(B, d, H, Lp, hd)[:, :, :, :L].transpose(0, 3, 1, 2, 4).reshape(B, S, H, hd)
    lse = lse.reshape(B, d, H, Lp)[:, :, :, :L].transpose(0, 3, 1, 2).reshape(B, S, H)
    return out, lse

def moba(q, k, v, bias_tab):
    B, S, H, hd = q.shape
    blk = MOBA_BLOCK
    nblk = -(-S // blk)
    Sp = nblk * blk
    scale = hd ** -0.5

    def prep(t):
        return jnp.pad(t, ((0, 0), (0, Sp - S), (0, 0), (0, 0))).transpose(0, 2, 1, 3)

    qt, kt, vt = prep(q), prep(k), prep(v)
    qb = qt.reshape(B, H, nblk, blk, hd)
    kb = kt.reshape(B, H, nblk, blk, hd)
    vb = vt.reshape(B, H, nblk, blk, hd)
    table_t = bias_tab.T.astype(jnp.float32)

    rel = jnp.arange(blk)[:, None] - jnp.arange(blk)[None, :]
    own_bias = bias_tab[t5_bucket(jnp.clip(rel, 0))].transpose(2, 0, 1).astype(jnp.float32)
    lo = jnp.einsum('bhnqc,bhnkc->bhnqk', qb, kb).astype(jnp.float32) * scale
    lo = jnp.where(rel >= 0, lo + own_bias[:, None], NEG_INF)
    m_own = jnp.max(lo, axis=-1)
    p_own = jnp.exp(lo - m_own[..., None])
    s_own = jnp.sum(p_own, axis=-1).reshape(B, H, Sp)
    acc_own = jnp.einsum('bhnqk,bhnkc->bhnqc', p_own, vb.astype(jnp.float32)).reshape(B, H, Sp, hd)
    m_own = m_own.reshape(B, H, Sp)

    kmean = jnp.mean(kb.astype(jnp.float32), axis=-2)
    gs = jnp.einsum('bhsc,bhnc->bhsn', qt.astype(jnp.float32), kmean)
    q_blk = jnp.arange(Sp) // blk
    gs = jnp.where(jnp.arange(nblk)[None, :] < q_blk[:, None], gs, NEG_INF)
    topk = min(MOBA_TOPK, nblk)
    _, sel = lax.top_k(gs, topk)
    sel_ok = jnp.arange(topk)[None, :] < q_blk[:, None]

    qc_n = MOBA_Q_CHUNK
    nc = Sp // qc_n
    xs = (qt.reshape(B, H, nc, qc_n, hd).transpose(2, 0, 1, 3, 4),
          sel.reshape(B, H, nc, qc_n, topk).transpose(2, 0, 1, 3, 4),
          sel_ok.reshape(nc, qc_n, topk),
          jnp.arange(Sp).reshape(nc, qc_n))
    b_i = jnp.arange(B)[:, None, None, None]
    h_i = jnp.arange(H)[None, :, None, None]

    def past_blocks(args):
        qc, ic, okc, pos = args
        kg = kb[b_i, h_i, ic]
        vg = vb[b_i, h_i, ic]
        lg = jnp.einsum('bhqc,bhqnjc->bhqnj', qc, kg).astype(jnp.float32) * scale
        dist = pos[None, None, :, None, None] - (ic[..., None] * blk + jnp.arange(blk))
        lg = jnp.where(okc[None, None, :, :, None], lg + table_t[h_i[..., None], t5_bucket(dist)], NEG_INF)
        lg = lg.reshape(B, H, qc_n, topk * blk)
        m = jnp.max(lg, axis=-1)
        p = jnp.exp(lg - m[..., None])
        s = jnp.sum(p, axis=-1)
        acc = jnp.einsum('bhqk,bhqkc->bhqc', p, vg.reshape(B, H, qc_n, topk * blk, hd).astype(jnp.float32))
        return acc, s, m

    acc_p, s_p, m_p = lax.map(past_blocks, xs)
    acc_p = acc_p.transpose(1, 2, 0, 3, 4).reshape(B, H, Sp, hd)
    s_p = s_p.transpose(1, 2, 0, 3).reshape(B, H, Sp)
    m_p = m_p.transpose(1, 2, 0, 3).reshape(B, H, Sp)

    m = jnp.maximum(m_own, m_p)
    a_o = jnp.exp(m_own - m)
    a_p = jnp.exp(m_p - m)
    out = (acc_own * a_o[..., None] + acc_p * a_p[..., None]) / (s_own * a_o + s_p * a_p)[..., None]
    return out[:, :, :S].transpose(0, 2, 1, 3).reshape(B, S, H * hd)

def cross_attention(h, m, w_q, w_kv, w_o):
    B, S, _ = h.shape
    M = m.shape[1]
    q = (h @ w_q).reshape(B, S, CROSS_HEADS, CROSS_HEAD_DIM)
    kv = (m @ w_kv).reshape(B, M, 2, CROSS_HEADS, CROSS_HEAD_DIM)
    lg = jnp.einsum('bshc,bmhc->bhsm', q, kv[:, :, 0]).astype(jnp.float32) * (CROSS_HEAD_DIM ** -0.5)
    p = jax.nn.softmax(lg, axis=-1)
    o = jnp.einsum('bhsm,bmhc->bshc', p, kv[:, :, 1].astype(jnp.float32)).reshape(B, S, CROSS_HEADS * CROSS_HEAD_DIM)
    return o.astype(h.dtype) @ w_o

def peer(h, w_q, sub_keys, u, v):
    B, S, D = h.shape
    T = B * S
    hf = h.reshape(T, D)
    q = (hf @ w_q).reshape(T, PEER_HEADS, 2, PEER_KEY_DIM // 2)
    sc = jnp.einsum('thpc,pkc->thpk', q, sub_keys).astype(jnp.float32)
    v1, i1 = lax.top_k(sc, PEER_TOPK)
    cand = (v1[:, :, 0, :, None] + v1[:, :, 1, None, :]).reshape(T, PEER_HEADS, PEER_TOPK * PEER_TOPK)
    cidx = (i1[:, :, 0, :, None] * PEER_N_KEYS + i1[:, :, 1, None, :]).reshape(T, PEER_HEADS, PEER_TOPK * PEER_TOPK)
    top, pos = lax.top_k(cand, PEER_TOPK)
    experts = jnp.take_along_axis(cidx, pos, axis=-1).reshape(T, PEER_HEADS * PEER_TOPK)
    gates = jax.nn.softmax(top, axis=-1).reshape(T, PEER_HEADS * PEER_TOPK)
    C = PEER_TOKEN_CHUNK
    nc = T // C

    def token_block(args):
        xc, ec, gc = args
        a = jax.nn.gelu(jnp.einsum('cd,ced->ce', xc, u[ec]).astype(jnp.float32), approximate=False)
        return jnp.einsum('ce,ced->cd', gc * a, v[ec].astype(jnp.float32))

    y = lax.map(token_block, (hf.reshape(nc, C, D), experts.reshape(nc, C, -1), gates.reshape(nc, C, -1)))
    return y.reshape(B, S, D).astype(h.dtype)

def setup_inputs(seed: int = 0) -> dict:
    key = jax.random.key(seed)
    ks = jax.random.split(key, 20)
    f32 = jnp.float32
    D = D_MODEL

    def nrm(k, shape, scale):
        return jax.random.normal(k, shape, f32) * scale

    def gain(k, shape):
        return 1.0 + 0.05 * jax.random.normal(k, shape, f32)

    wa = DIL_HEADS * HEAD_DIM
    wb = MOBA_HEADS * HEAD_DIM
    wc = CROSS_HEADS * CROSS_HEAD_DIM
    return {
        'x': nrm(ks[0], (BATCH, SEQ, D), 1.0),
        'mem': nrm(ks[1], (BATCH, N_MEM, D), 1.0),
        'rel_bias': nrm(ks[2], (REL_BUCKETS, N_SELF_HEADS), 0.5),
        'g_mix': gain(ks[3], (DEPTH, D)),
        'w_in': nrm(ks[4], (DEPTH, D, IN_COLS), D ** -0.5),
        'b_gate': nrm(ks[5], (DEPTH, GATE_WIDTH), 0.02),
        'w_branch_a': nrm(ks[6], (DEPTH, wa, D), wa ** -0.5),
        'w_branch_b': nrm(ks[7], (DEPTH, wb, D), wb ** -0.5),
        'w_out': nrm(ks[8], (DEPTH, D, D), D ** -0.5),
        'g_cross': gain(ks[9], (DEPTH, D)),
        'g_mem': gain(ks[10], (DEPTH, D)),
        'w_q_cross': nrm(ks[11], (DEPTH, D, wc), D ** -0.5),
        'w_kv_cross': nrm(ks[12], (DEPTH, D, 2 * wc), D ** -0.5),
        'w_o_cross': nrm(ks[13], (DEPTH, wc, D), wc ** -0.5),
        'g_ffn': gain(ks[14], (DEPTH, D)),
        'w_q_peer': nrm(ks[15], (DEPTH, D, PEER_HEADS * PEER_KEY_DIM), D ** -0.5),
        'peer_sub_keys': nrm(ks[16], (DEPTH, 2, PEER_N_KEYS, PEER_KEY_DIM // 2), (PEER_KEY_DIM // 2) ** -0.5),
        'peer_u': nrm(ks[17], (DEPTH, PEER_N_EXPERTS, D), D ** -0.5),
        'peer_v': nrm(ks[18], (DEPTH, PEER_N_EXPERTS, D), 0.5),
        'g_final': gain(ks[19], (D,)),
    }

def reference(x, mem, rel_bias, g_mix, w_in, b_gate, w_branch_a, w_branch_b, w_out,
              g_cross, g_mem, w_q_cross, w_kv_cross, w_o_cross,
              g_ffn, w_q_peer, peer_sub_keys, peer_u, peer_v, g_final):
    B, S, D = x.shape
    for l in range(DEPTH):
        h = rmsnorm(x, g_mix[l])
        proj = h @ w_in[l]
        p_dil = proj[..., :DIL_WIDTH].reshape(B, S, N_DIL_GROUPS, 3, DIL_HEADS, HEAD_DIM)
        p_moba = proj[..., DIL_WIDTH:DIL_WIDTH + MOBA_WIDTH].reshape(B, S, 3, MOBA_HEADS, HEAD_DIM)
        p_gate = proj[..., DIL_WIDTH + MOBA_WIDTH:] + b_gate[l]
        outs = []
        lses = []
        for gi, (win, dil) in enumerate(DIL_GROUPS):
            o, s = dilated_group(p_dil[:, :, gi, 0], p_dil[:, :, gi, 1], p_dil[:, :, gi, 2], win, dil,
                                 rel_bias[:, gi * DIL_HEADS:(gi + 1) * DIL_HEADS])
            outs.append(o)
            lses.append(s)
        wgt = jax.nn.softmax(jnp.stack(lses, axis=0), axis=0)
        o_dil = jnp.sum(wgt[..., None] * jnp.stack(outs, axis=0), axis=0).reshape(B, S, DIL_HEADS * HEAD_DIM).astype(x.dtype)
        o_moba = moba(p_moba[:, :, 0], p_moba[:, :, 1], p_moba[:, :, 2],
                      rel_bias[:, N_DIL_GROUPS * DIL_HEADS:]).astype(x.dtype)
        gates = jax.nn.sigmoid(p_gate.astype(jnp.float32)).astype(x.dtype).reshape(B, S, 2, D)
        merged = gates[:, :, 0] * (o_dil @ w_branch_a[l]) + gates[:, :, 1] * (o_moba @ w_branch_b[l])
        x = x + merged @ w_out[l]
        x = x + cross_attention(rmsnorm(x, g_cross[l]), rmsnorm(mem, g_mem[l]),
                                w_q_cross[l], w_kv_cross[l], w_o_cross[l])
        x = x + peer(rmsnorm(x, g_ffn[l]), w_q_peer[l], peer_sub_keys[l], peer_u[l], peer_v[l])
    return rmsnorm(x, g_final)


_drawn_inputs = setup_inputs


def setup_inputs(seed=0):
    import zlib

    import numpy as np

    out = dict(_drawn_inputs(seed))
    spreads = {}
    factors = {'b_gate': 5.849, 'g_cross': 2.932}
    for name, (base, spread) in spreads.items():
        noise = np.random.default_rng([zlib.crc32(name.encode()), seed]).standard_normal(out[name].shape)
        drawn = base * np.exp(spread * noise) if base else spread * noise
        out[name] = jnp.asarray(drawn.astype(out[name].dtype))
    for name, factor in factors.items():
        out[name] = (out[name] * factor).astype(out[name].dtype)
    return out
```

```python
from contextlib import ExitStack

import numpy as np

import concourse.bass as bass
from concourse import mybir

ALU = mybir.AluOpType
ACT = mybir.ActivationFunctionType
AX = mybir.AxisListType
F32 = mybir.dt.float32
U32 = mybir.dt.uint32

P = 128
D = 1024
S = 256
TILES = S // P
CHUNKS = D // P
HEAD_DIM = 64
DIL_HEADS, DIL_GROUPS = 4, 3
MOBA_HEADS = 8
SELF_HEADS = DIL_HEADS * DIL_GROUPS + MOBA_HEADS
SOFTMAXES = DIL_HEADS + MOBA_HEADS
CROSS_HEADS, CROSS_DIM = 4, 128
PEER_HEADS, PEER_KEYS, TOPK = 8, 128, 16
EPS = 1e-6
MASKED = -1e30
LINE = 383
LINE_PAD = 384

PAIR_ROWS = [(0, 1, 16), (1, 1, 8), (2, 1, 5), (3, 1, 4), (4, 1, 3), (5, 3, 2), (8, 8, 1)]
PAIRS = sum(n * w for _, n, w in PAIR_ROWS)

PANEL = 2048
PANELS = ([f"kv{j}" for j in range(4)] + [f"qkv{j}" for j in range(15)] + [f"gate{j}" for j in range(8)]
          + ["branch_a", "branch_b0", "branch_b1"] + [f"out{j}" for j in range(4)]
          + [f"qcross{j}" for j in range(2)] + [f"ocross{j}" for j in range(2)]
          + [f"qpeer{j}" for j in range(PEER_HEADS)])
PANEL_RING = 6
RING = 8
GROUP = 2
DIAGS = 8
BANKS = 4


def self_softmax_heads(r):
    if r < DIL_HEADS:
        return [g * DIL_HEADS + r for g in range(DIL_GROUPS)]
    return [DIL_HEADS * DIL_GROUPS + r - DIL_HEADS]


def self_slots(r):
    if r < DIL_HEADS:
        return [r * DIL_GROUPS + g for g in range(DIL_GROUPS)]
    return [DIL_HEADS * DIL_GROUPS + r - DIL_HEADS]


def product_order():
    order = []

    def add(name, engine):
        order.append((name, engine))

    add("keys", "act")
    for stage in ("mem", "mix"):
        for c in range(4):
            add(f"turn_{stage}{c}", ("act", "dve")[c % 2])
    add("line", "dve")
    for j in range(4):
        add(f"kv{j}", ("act", "dve")[j % 2])
    for j in range(15):
        add(f"qkv{j}", ("act", "dve")[j % 2])
    for r in range(SOFTMAXES):
        for s in self_slots(r):
            add(f"score{s}", "dve")
    for j in range(8):
        add(f"gate{j}", "act")
    for r in range(SOFTMAXES + 1):
        if r < SOFTMAXES:
            for s in self_slots(r):
                add(f"probs_t{s}", ("act", "dve")[s % 2])
        if r >= 1:
            add(f"self_o{r - 1}", ("act", "dve")[r % 2])
    for c in range(CHUNKS):
        add(f"branch{c}", "dve")
    for j in range(4):
        add(f"out{j}", "dve")
    for c in range(4):
        add(f"turn_cross{c}", ("act", "dve")[c % 2])
    for j in range(2):
        add(f"qcross{j}", ("act", "dve")[j % 2])
    for h in range(CROSS_HEADS):
        add(f"cross_score{h}", "act")
    for h in range(CROSS_HEADS + 1):
        if h < CROSS_HEADS:
            add(f"cross_probs_t{h}", "dve")
        if h >= 1:
            add(f"cross_o{h - 1}", "act")
    for j in range(2):
        for t in range(TILES):
            add(f"ocross{j}_{t}", "dve")
    for c in range(4):
        add(f"turn_ffn{c}", ("act", "dve")[c % 2])
    for h in range(PEER_HEADS + 1):
        if h < PEER_HEADS:
            add(f"qpeer{h}", "act")
        if h >= 1:
            add(f"key_score{h - 1}", "act")
    return order


PRODUCTS = product_order()
PLACE = {name: n for n, (name, _) in enumerate(PRODUCTS)}
TAKER = dict(PRODUCTS)


def taken_count(name):
    return sum(1 for _, e in PRODUCTS[:PLACE[name] + 1] if e == TAKER[name])


def last_product_of_panel(panel):
    if panel == "branch_a" or panel == "branch_b1":
        return f"branch{CHUNKS - 1}"
    if panel == "branch_b0":
        return f"branch{CHUNKS // 2 - 1}"
    if panel.startswith("ocross"):
        return panel + f"_{TILES - 1}"
    return panel


def build(nc, x_in, mem_in, rel_bias, panels, keys_in, experts, gain_cols, gain_rows, ident_in,
          onehot_in, mask_in, iota_in, out):
    with ExitStack() as ctx:
        def sb(name, shape, dt=F32):
            return ctx.enter_context(nc.sbuf_tensor(name, shape, dt))

        def sem(name):
            return ctx.enter_context(nc.semaphore(name))

        line_dram = nc.dram_tensor("line_scratch", [P, SELF_HEADS, LINE_PAD], F32)

        x = sb("x", [P, TILES, D])
        hT = sb("hT", [P, CHUNKS, S])
        weights = sb("weights", [P, PANEL_RING, PANEL])
        ident = sb("ident", [P, P])
        gains = sb("gains", [P, 48])
        half_b = sb("half_b", [P, 16])
        iota = sb("iota", [P, PAIRS])
        ckT = sb("ckT", [P, CROSS_HEADS, S])
        cV = sb("cV", [P, TILES, CROSS_HEADS * CROSS_DIM])
        oT = sb("oT", [P, 6, S])
        probsT = sb("probsT", [P, 8, 384])
        keysT = sb("keysT", [P, 2, PEER_KEYS])
        qpT = sb("qpT", [P, 2, 2, S])
        tmpA = sb("tmpA", [P, 2, S])
        tmpB = sb("tmpB", [P, 2, S])
        neg_max = sb("neg_max", [P, SOFTMAXES, TILES])
        row_max = sb("row_max", [P, SOFTMAXES, TILES])
        row_sum = sb("row_sum", [P, SOFTMAXES, TILES])
        row_inv = sb("row_inv", [P, SOFTMAXES, TILES])
        c_max = sb("c_max", [P, CROSS_HEADS, TILES])
        c_neg = sb("c_neg", [P, CROSS_HEADS, TILES])
        c_sum = sb("c_sum", [P, CROSS_HEADS, TILES])
        c_inv = sb("c_inv", [P, CROSS_HEADS, TILES])
        sumsq = sb("sumsq", [P, 5, TILES])
        meansq = sb("meansq", [P, 5, TILES])
        root = sb("root", [P, 5, TILES])
        rstd = sb("rstd", [P, 5, TILES])
        key_cur = sb("key_cur", [P, 2, PEER_KEYS])
        key_rest = sb("key_rest", [P, 2, PEER_KEYS])
        ranked = sb("ranked", [P, 2, 2, TOPK])
        ranked_i = sb("ranked_i", [P, 2, TOPK], U32)
        pairs = sb("pairs", [P, 2, PAIRS])
        pairs_rest = sb("pairs_rest", [P, PAIRS])
        top = sb("top", [P, TOPK])
        top_at = sb("top_at", [P, TOPK], U32)
        top_atf = sb("top_atf", [P, TOPK])
        pick = sb("pick", [P, TOPK, PAIRS])
        expert_f = sb("expert_f", [P, TOPK])
        expert = sb("expert", [P, 2, TOPK], U32)
        neg_top = sb("neg_top", [P, 1])
        top_exp = sb("top_exp", [P, TOPK])
        top_sum = sb("top_sum", [P, 1])
        top_inv = sb("top_inv", [P, 1])
        gate = sb("gate", [P, TOPK])
        dots = sb("dots", [P, TOPK])
        acts = sb("acts", [P, TOPK])
        diag = sb("diag", [P, DIAGS, P])

        arena = sb("arena", [P, 24576])

        def part(at, *shape):
            n = int(np.prod(shape))
            flat = arena[:, at:at + n]
            if len(shape) == 1:
                return flat
            names = "abc"[:len(shape)]
            return flat.rearrange(f"p ({' '.join(names)}) -> p {' '.join(names)}",
                                  **{k: v for k, v in zip(names, shape)})

        qT = part(0, SELF_HEADS // 2, S)
        kT = part(2560, SELF_HEADS // 2, S)
        vv = part(5120, TILES, SELF_HEADS * HEAD_DIM)
        bias = part(7680, SELF_HEADS, S)
        probs = part(12800, SELF_HEADS, 384)
        gates = part(20480, 2 * CHUNKS, S)
        mem_xn = part(12800, TILES, D)
        mem_rows = part(14848, TILES, D)
        mix_xn = part(16896, TILES, D)
        line = part(18944, LINE_PAD)
        line_mask = part(19328, LINE_PAD)
        onehot = part(19712, LINE_PAD)
        rel_sb = part(20096, SELF_HEADS)
        keys_rows = part(20160, 2, PEER_KEYS)
        memT = part(20480, CHUNKS, S)
        qcT = part(0, CROSS_HEADS, S)
        c_probs = part(1024, CROSS_HEADS, TILES * S)
        c_probsT = part(3072, 2, TILES * S)
        ocT = part(4096, CROSS_HEADS, S)
        cross_xn = part(5120, TILES, D)
        ffn_xn = part(7168, TILES, D)
        ring = part(0, RING, 2 * D)
        scores = arena[:, 16384:16384 + TILES * PEER_HEADS * 2 * PEER_KEYS]
        h_rows = part(20480, TILES, D)
        g_ffn_row = part(22528, D)
        g_final_row = part(23552, D)

        ps = ctx.enter_context(nc.psum_tensor("ps", [P, BANKS, 512], F32))
        y = ctx.enter_context(nc.psum_tensor("y", [P, TILES, D], F32))

        small_in = sem("small_in")
        x_loaded = sem("x_loaded")
        mem_loaded = sem("mem_loaded")
        panel_in = [sem(f"panel_in{i}") for i in range(PANEL_RING)]
        line_out = sem("line_out")
        bias_in = sem("bias_in")
        rows_in = sem("rows_in")
        product_ready = sem("product_ready")
        taken = {"act": sem("taken_act"), "dve": sem("taken_dve")}
        sumsq_ready = sem("sumsq_ready")
        meansq_ready = sem("meansq_ready")
        root_ready = sem("root_ready")
        rstd_ready = sem("rstd_ready")
        xn_ready = sem("xn_ready")
        half_b_ready = sem("half_b_ready")
        line_ready = sem("line_ready")
        logits_ready = sem("logits_ready")
        row_max_ready = sem("row_max_ready")
        neg_max_ready = sem("neg_max_ready")
        exp_ready = sem("exp_ready")
        row_inv_ready = sem("row_inv_ready")
        probs_ready = sem("probs_ready")
        gates_tanh = sem("gates_tanh")
        gates_ready = sem("gates_ready")
        gated = sem("gated")
        merged_ready = sem("merged_ready")
        x_ready = sem("x_ready")
        c_max_ready = sem("c_max_ready")
        c_neg_ready = sem("c_neg_ready")
        c_exp_ready = sem("c_exp_ready")
        c_inv_ready = sem("c_inv_ready")
        c_probs_ready = sem("c_probs_ready")
        h_rows_ready = sem("h_rows_ready")
        route_step = sem("route_step")
        top_ready = sem("top_ready")
        top_exp_ready = sem("top_exp_ready")
        gate_step = sem("gate_step")
        experts_ready = sem("experts_ready")
        slot_in = [sem(f"slot_in{i}") for i in range(RING)]
        slot_free = sem("slot_free")
        dots_ready = sem("dots_ready")
        acts_ready = sem("acts_ready")
        diag_ready = sem("diag_ready")
        y_ready = sem("y_ready")
        final_ready = sem("final_ready")
        out_done = sem("out_done")

        def bank(name):
            return ps[:, PLACE[name] % BANKS, :]

        def panel_sb(n):
            return weights[:, n % PANEL_RING, :]

        NORM = {"mem": 0, "mix": 1, "cross": 2, "ffn": 3, "final": 4}
        UNITS = TILES * PEER_HEADS
        SMALL = 7

        def wait_apart(eng, semaphore, value):
            eng.wait_ge(semaphore, value)
            eng.nop(nofuse=True)

        block = ctx.enter_context(nc.Block())

        @block.sync
        def _(sp):
            sp.dma_start(mem_rows, mem_in.rearrange("b (t p) d -> p (b t) d", p=P)).then_inc(mem_loaded, 16)
            sp.dma_start(x[:], x_in.rearrange("b (t p) d -> p (b t) d", p=P)).then_inc(x_loaded, 16)
            sp.dma_start(ident[:], ident_in).then_inc(small_in, 16)
            sp.dma_start(gains[:], gain_cols).then_inc(small_in, 16)
            sp.dma_start(iota[:], iota_in).then_inc(small_in, 16)
            sp.dma_start(rel_sb[0:rel_bias.shape[0]], rel_bias).then_inc(small_in, 16)
            sp.dma_start(onehot[0:rel_bias.shape[0]], onehot_in).then_inc(small_in, 16)
            sp.dma_start(line_mask[0:SELF_HEADS], mask_in).then_inc(small_in, 16)
            sp.dma_start(keys_rows, keys_in.rearrange("p k c -> k p c")).then_inc(small_in, 16)
            for n, name in enumerate(PANELS):
                if n >= PANEL_RING:
                    sp.wait_ge(product_ready, PLACE[last_product_of_panel(PANELS[n - PANEL_RING])] + 1)
                sp.dma_start(panel_sb(n), panels[n]).then_inc(panel_in[n % PANEL_RING], 16)
                if n == PANEL_RING - 1:
                    sp.wait_ge(line_ready, 1)
                    sp.dma_start(line_dram.ap().rearrange("q h c -> h q c"),
                                 line[0:SELF_HEADS].unsqueeze(1).to_broadcast([SELF_HEADS, P, LINE_PAD])
                                 ).then_inc(line_out, 16)
                    sp.wait_ge(line_out, 16)
                    sp.dma_start(bias, bass.AP(line_dram, P - 1, [[SELF_HEADS * LINE_PAD - 1, P],
                                                                  [LINE_PAD, SELF_HEADS], [1, S]])
                                 ).then_inc(bias_in, 16)
                if name == "qpeer0":
                    sp.wait_ge(merged_ready, CHUNKS)
                    sp.dma_start(g_ffn_row, gain_rows[0:1].to_broadcast([P, D])).then_inc(rows_in, 16)
                    sp.dma_start(g_final_row, gain_rows[1:2].to_broadcast([P, D])).then_inc(rows_in, 16)
            for t in range(TILES):
                sp.wait_ge(final_ready, t + 1)
                sp.dma_start(out[0, t * P:(t + 1) * P, :], x[:, t, :]).then_inc(out_done, 16)
            sp.wait_ge(out_done, 16 * TILES)

        @block.tensor
        def _(pe):
            def begin(name):
                n = PLACE[name]
                if n >= BANKS:
                    before = PRODUCTS[n - BANKS][0]
                    pe.wait_ge(taken[TAKER[before]], taken_count(before))
                return bank(name)

            def panel(name):
                n = PANELS.index(name)
                pe.wait_ge(panel_in[n % PANEL_RING], 16 * (n // PANEL_RING + 1))
                return panel_sb(n)

            def turn(stage, xn, scaled):
                pe.wait_ge(xn_ready, scaled)
                for c in range(4):
                    b = begin(f"turn_{stage}{c}")
                    for k in range(2):
                        for t in range(TILES):
                            mm = pe.transpose(b[:, k * S + t * P:k * S + (t + 1) * P],
                                              xn[:, t, (2 * c + k) * P:(2 * c + k + 1) * P], ident[:])
                    mm.then_inc(product_ready, 1)

            def channels_by_tokens(name, srcT):
                w = panel(name)
                b = begin(name)
                for blk in range(2):
                    for k in range(CHUNKS):
                        mm = pe.matmul(b[:, blk * S:(blk + 1) * S],
                                       w[:, k * S + blk * P:k * S + (blk + 1) * P], srcT[:, k, :],
                                       start=(k == 0), stop=(k == CHUNKS - 1))
                mm.then_inc(product_ready, 1)

            def tokens_by_channels(name, srcT):
                w = panel(name)
                b = begin(name)
                for t in range(TILES):
                    for k in range(CHUNKS):
                        mm = pe.matmul(b[:, t * S:(t + 1) * S], srcT[:, k, t * P:(t + 1) * P],
                                       w[:, k * S:(k + 1) * S], start=(k == 0), stop=(k == CHUNKS - 1))
                mm.then_inc(product_ready, 1)

            def all_taken(name):
                upto = PRODUCTS[:PLACE[name] + 1]
                for e in ("act", "dve"):
                    pe.wait_ge(taken[e], sum(1 for _, f in upto if f == e))

            pe.wait_ge(small_in, 16 * SMALL)
            b = begin("keys")
            for p in range(2):
                mm = pe.transpose(b[:, p * P:(p + 1) * P], keys_rows[:, p, :], ident[:])
            mm.then_inc(product_ready, 1)
            turn("mem", mem_xn, 1)
            turn("mix", mix_xn, 2)
            nb = rel_bias.shape[0]
            b = begin("line")
            pe.matmul(b[0:SELF_HEADS, 0:LINE_PAD], rel_sb[0:nb], onehot[0:nb],
                      start=True, stop=True).then_inc(product_ready, 1)

            all_taken("turn_mem3")
            for j in range(2):
                channels_by_tokens(f"kv{j}", memT)
            for j in range(2, 4):
                tokens_by_channels(f"kv{j}", memT)
            all_taken("turn_mix3")
            for j in range(15):
                if j in VALUE_PANELS:
                    tokens_by_channels(f"qkv{j}", hT)
                else:
                    channels_by_tokens(f"qkv{j}", hT)
            all_taken("qkv14")
            for r in range(SOFTMAXES):
                for s, head in zip(self_slots(r), self_softmax_heads(r)):
                    b = begin(f"score{s}")
                    lo = HEAD_DIM * (head % 2)
                    q = qT[lo:lo + HEAD_DIM, head // 2, :]
                    k = kT[lo:lo + HEAD_DIM, head // 2, :]
                    pe.matmul(b[:, 0:P], q[:, 0:P], k[:, 0:P], start=True, stop=True)
                    pe.matmul(b[:, P:3 * P], q[:, P:S], k, start=True, stop=True).then_inc(product_ready, 1)
            for j in range(8):
                channels_by_tokens(f"gate{j}", hT)
            turned = 0
            for r in range(SOFTMAXES + 1):
                if r < SOFTMAXES:
                    pe.wait_ge(probs_ready, r + 1)
                    for s in self_slots(r):
                        b = begin(f"probs_t{s}")
                        for i in range(3):
                            mm = pe.transpose(b[:, i * P:(i + 1) * P], probs[:, s, i * P:(i + 1) * P], ident[:])
                        mm.then_inc(product_ready, 1)
                if r >= 1:
                    b = begin(f"self_o{r - 1}")
                    all_taken(f"probs_t{self_slots(r - 1)[-1]}")
                    lo = HEAD_DIM * ((r - 1) % 2)
                    heads = self_softmax_heads(r - 1)
                    for i, head in enumerate(heads):
                        pt = probsT[:, self_slots(r - 1)[i] % 8, :]
                        v = vv[:, :, head * HEAD_DIM:(head + 1) * HEAD_DIM]
                        pe.matmul(b[lo:lo + HEAD_DIM, 0:S], v[:, 0, :], pt[:, 0:S], start=(i == 0), stop=False)
                        mm = pe.matmul(b[lo:lo + HEAD_DIM, P:S], v[:, 1, :], pt[:, S:3 * P],
                                       start=False, stop=(i == len(heads) - 1))
                    mm.then_inc(product_ready, 1)
            all_taken(f"self_o{SOFTMAXES - 1}")
            wa = panel("branch_a")
            for c in range(CHUNKS):
                wb = panel(f"branch_b{c // 4}")
                b = begin(f"branch{c}")
                for k in range(2):
                    pe.matmul(b[:, 0:S], wa[:, k * D + c * P:k * D + (c + 1) * P], oT[:, k, :],
                              start=(k == 0), stop=(k == 1))
                for k in range(4):
                    mm = pe.matmul(b[:, S:2 * S], wb[:, k * 512 + (c % 4) * P:k * 512 + (c % 4 + 1) * P],
                                   oT[:, 2 + k, :], start=(k == 0), stop=(k == 3))
                mm.then_inc(product_ready, 1)
            pe.wait_ge(merged_ready, CHUNKS)
            for j in range(4):
                tokens_by_channels(f"out{j}", hT)
            turn("cross", cross_xn, 3)
            all_taken("turn_cross3")
            for j in range(2):
                channels_by_tokens(f"qcross{j}", hT)
            all_taken("qcross1")
            for h in range(CROSS_HEADS):
                b = begin(f"cross_score{h}")
                for t in range(TILES):
                    mm = pe.matmul(b[:, t * S:(t + 1) * S], qcT[:, h, t * P:(t + 1) * P], ckT[:, h, :],
                                   start=True, stop=True)
                mm.then_inc(product_ready, 1)
            for h in range(CROSS_HEADS + 1):
                if h < CROSS_HEADS:
                    b = begin(f"cross_probs_t{h}")
                    pe.wait_ge(c_probs_ready, h + 1)
                    for m in range(TILES):
                        for t in range(TILES):
                            mm = pe.transpose(b[:, m * S + t * P:m * S + (t + 1) * P],
                                              c_probs[:, h, t * S + m * P:t * S + (m + 1) * P], ident[:])
                    mm.then_inc(product_ready, 1)
                if h >= 1:
                    b = begin(f"cross_o{h - 1}")
                    all_taken(f"cross_probs_t{h - 1}")
                    for m in range(TILES):
                        mm = pe.matmul(b[:, 0:S], cV[:, m, (h - 1) * P:h * P],
                                       c_probsT[:, (h - 1) % 2, m * S:(m + 1) * S],
                                       start=(m == 0), stop=(m == TILES - 1))
                    mm.then_inc(product_ready, 1)
            all_taken(f"cross_o{CROSS_HEADS - 1}")
            for j in range(2):
                w = panel(f"ocross{j}")
                for t in range(TILES):
                    b = begin(f"ocross{j}_{t}")
                    for k in range(CROSS_HEADS):
                        mm = pe.matmul(b, ocT[:, k, t * P:(t + 1) * P], w[:, k * 512:(k + 1) * 512],
                                       start=(k == 0), stop=(k == CROSS_HEADS - 1))
                    mm.then_inc(product_ready, 1)
            turn("ffn", ffn_xn, 4)
            all_taken("turn_ffn3")
            for t in range(TILES):
                for half in range(2):
                    mm = pe.matmul(y[:, t, half * 512:(half + 1) * 512], ident[:],
                                   x[:, t, half * 512:(half + 1) * 512], start=True, stop=False,
                                   skip_group_check=True)
            mm.then_inc(slot_free, RING)
            for h in range(PEER_HEADS + 1):
                if h < PEER_HEADS:
                    channels_by_tokens(f"qpeer{h}", hT)
                if h >= 1:
                    b = begin(f"key_score{h - 1}")
                    all_taken(f"qpeer{h - 1}")
                    for t in range(TILES):
                        for p in range(2):
                            mm = pe.matmul(b[:, (2 * t + p) * P:(2 * t + p + 1) * P],
                                           qpT[:, (h - 1) % 2, p, t * P:(t + 1) * P], keysT[:, p, :],
                                           start=True, stop=True)
                    mm.then_inc(product_ready, 1)

            def use_slots(u, t):
                for s in range(TOPK):
                    if s % GROUP == 0:
                        pe.wait_ge(diag_ready, u * (TOPK // GROUP) + (s // GROUP + 1))
                    for half in range(2):
                        at = D + half * 512
                        mm = pe.matmul(y[:, t, half * 512:(half + 1) * 512], diag[:, s % DIAGS, :],
                                       ring[:, s % RING, at:at + 512], start=False, stop=False,
                                       skip_group_check=True)
                    mm.then_inc(slot_free, 1)

            for t in range(TILES):
                with pe.Fori(0, PEER_HEADS) as h:
                    use_slots(h + t * PEER_HEADS, t)

        @block.scalar
        def _(act):
            def take(name):
                act.wait_ge(product_ready, PLACE[name] + 1)
                return bank(name)

            def took(instruction):
                instruction.then_inc(taken["act"], 1)

            def squares(stage, rows, junk):
                n = NORM[stage]
                for t in range(TILES):
                    nc.scalar.activation(junk[:, t, :], rows[:, t, :], ACT.Square,
                                         accum_out=sumsq[:, n, t:t + 1]).then_inc(sumsq_ready, 1)

            def roots(stage):
                n = NORM[stage]
                act.wait_ge(meansq_ready, n + 1)
                nc.scalar.activation(root[:, n, :], meansq[:, n, :], ACT.Sqrt).then_inc(root_ready, 1)

            def turned(stage, dst, gain):
                for c in range(0, 4, 2):
                    b = take(f"turn_{stage}{c}")
                    for k in range(2):
                        i = nc.scalar.activation(dst[:, 2 * c + k, :], b[:, k * S:(k + 1) * S], ACT.Copy,
                                                 scale=gains[:, gain + 2 * c + k:gain + 2 * c + k + 1])
                    took(i)

            act.wait_ge(mem_loaded, 16)
            squares("mem", mem_rows, mem_xn)
            act.wait_ge(x_loaded, 16)
            squares("mix", x, mix_xn)
            roots("mem")
            roots("mix")
            b = take("keys")
            took(nc.scalar.copy(keysT[:].rearrange("p a b -> p (a b)"), b[:, 0:2 * P]))
            turned("mem", memT, 0)
            turned("mix", hT, CHUNKS)
            for j in range(0, 4, 2):
                b = take(f"kv{j}")
                took(copy_kv(nc.scalar.copy, j, b, ckT, cV))
            for j in range(0, 15, 2):
                b = take(f"qkv{j}")
                took(copy_qkv(nc.scalar.copy, j, b, qT, kT, vv))
            act.wait_ge(half_b_ready, 1)
            for r in range(SOFTMAXES):
                s0, n = self_slots(r)[0], len(self_slots(r))
                act.wait_ge(neg_max_ready, r + 1)
                for t in range(TILES):
                    pr = probs[:, s0:s0 + n, t * P:t * P + (t + 1) * P]
                    i = nc.scalar.activation(pr, pr, ACT.Exp, bias=neg_max[:, r, t:t + 1],
                                             accum_out=row_sum[:, r, t:t + 1])
                i.then_inc(exp_ready, 1)
            for j in range(8):
                b = take(f"gate{j}")
                for k in range(2):
                    i = nc.scalar.activation(gates[:, 2 * j + k, :], b[:, k * S:(k + 1) * S], ACT.Tanh,
                                             bias=half_b[:, 2 * j + k:2 * j + k + 1], scale=0.5)
                took(i)
            for r in range(SOFTMAXES + 1):
                if r < SOFTMAXES:
                    for s in self_slots(r):
                        if TAKER[f"probs_t{s}"] == "act":
                            b = take(f"probs_t{s}")
                            took(nc.scalar.copy(probsT[:, s % 8, :], b[:, 0:384]))
                if r >= 1 and TAKER[f"self_o{r - 1}"] == "act":
                    b = take(f"self_o{r - 1}")
                    took(copy_self_o(nc.scalar.copy, r - 1, b, oT))
            act.wait_ge(x_ready, 4)
            squares("cross", x, cross_xn)
            roots("cross")
            turned("cross", hT, 2 * CHUNKS)
            b = take("qcross0")
            took(nc.scalar.copy(qcT[:, 0:2, :].rearrange("p a b -> p (a b)"), b))
            for h in range(CROSS_HEADS):
                b = take(f"cross_score{h}")
                act.wait_ge(c_neg_ready, h + 1)
                for t in range(TILES):
                    i = nc.scalar.activation(c_probs[:, h, t * S:(t + 1) * S], b[:, t * S:(t + 1) * S], ACT.Exp,
                                             bias=c_neg[:, h, t:t + 1], scale=CROSS_DIM ** -0.5,
                                             accum_out=c_sum[:, h, t:t + 1])
                took(i)
            for h in range(CROSS_HEADS):
                b = take(f"cross_o{h}")
                took(nc.scalar.copy(ocT[:, h, :], b[:, 0:S]))
            act.wait_ge(x_ready, 8)
            squares("ffn", x, ffn_xn)
            roots("ffn")
            turned("ffn", hT, 3 * CHUNKS)
            by_unit = scores.rearrange("p (t h k) -> p t h k", t=TILES, h=PEER_HEADS)
            for h in range(PEER_HEADS + 1):
                if h < PEER_HEADS:
                    b = take(f"qpeer{h}")
                    took(nc.scalar.copy(qpT[:, h % 2, :, :].rearrange("p a b -> p (a b)"), b))
                if h >= 1:
                    b = take(f"key_score{h - 1}")
                    took(nc.scalar.copy(by_unit[:, :, h - 1, :], b.rearrange("p (t k) -> p t k", t=TILES)))

            def expert_softmax(n):
                act.wait_ge(top_ready, n)
                nc.scalar.activation(top_exp[:], top[:], ACT.Exp, bias=neg_top[:, 0:1],
                                     accum_out=top_sum[:, 0:1]).then_inc(top_exp_ready, 1)

            def gelus(u):
                for g in range(TOPK // GROUP):
                    act.wait_ge(dots_ready, u * (TOPK // GROUP) + (g + 1))
                    nc.scalar.activation(acts[:, g * GROUP:(g + 1) * GROUP], dots[:, g * GROUP:(g + 1) * GROUP],
                                         ACT.Gelu).then_inc(acts_ready, 1)

            expert_softmax(1)
            with act.Fori(0, UNITS - 1) as u:
                expert_softmax(u + 2)
                gelus(u)
            gelus(UNITS - 1)
            act.wait_ge(y_ready, 1)
            squares("final", y, x)
            roots("final")

        @block.vector
        def _(dve):
            def take(name):
                dve.wait_ge(product_ready, PLACE[name] + 1)
                return bank(name)

            def took(instruction):
                instruction.then_inc(taken["dve"], 1)

            def inverse_roots(stage):
                n = NORM[stage]
                dve.wait_ge(sumsq_ready, TILES * (n + 1))
                nc.vector.tensor_scalar(meansq[:, n, :], sumsq[:, n, :], 1.0 / D, EPS, ALU.mult, ALU.add
                                        ).then_inc(meansq_ready, 1)
                dve.wait_ge(root_ready, n + 1)
                nc.vector.reciprocal(rstd[:, n, :], root[:, n, :]).then_inc(rstd_ready, 1)
                dve.wait_ge(rstd_ready, n + 1)

            def normalise(stage, rows, xn):
                inverse_roots(stage)
                for t in range(TILES):
                    i = nc.vector.tensor_scalar(xn[:, t, :], rows[:, t, :], rstd[:, NORM[stage], t:t + 1], None,
                                                ALU.mult)
                i.then_inc(xn_ready, 1)

            def turned(stage, dst, gain):
                for c in range(1, 4, 2):
                    b = take(f"turn_{stage}{c}")
                    for k in range(2):
                        i = nc.vector.tensor_scalar(dst[:, 2 * c + k, :], b[:, k * S:(k + 1) * S],
                                                    gains[:, gain + 2 * c + k:gain + 2 * c + k + 1], None, ALU.mult)
                    took(i)

            normalise("mem", mem_rows, mem_xn)
            normalise("mix", x, mix_xn)
            dve.wait_ge(small_in, 16 * SMALL)
            nc.vector.tensor_scalar(half_b[:], gains[:, 32:48], 0.5, None, ALU.mult).then_inc(half_b_ready, 1)
            turned("mem", memT, 0)
            turned("mix", hT, CHUNKS)
            b = take("line")
            i = nc.vector.tensor_tensor(line[0:SELF_HEADS], b[0:SELF_HEADS, 0:LINE_PAD], line_mask[0:SELF_HEADS],
                                        ALU.add)
            i.then_inc(line_ready, 1)
            dve.wait_ge(line_ready, 1)
            took(nc.vector.tensor_copy(half_b[:, 0:1], half_b[:, 0:1]))
            for j in range(1, 4, 2):
                b = take(f"kv{j}")
                took(copy_kv(nc.vector.tensor_copy, j, b, ckT, cV))
            for j in range(1, 15, 2):
                b = take(f"qkv{j}")
                took(copy_qkv(nc.vector.tensor_copy, j, b, qT, kT, vv))

            def self_inverse(r):
                dve.wait_ge(exp_ready, r + 1)
                nc.vector.reciprocal(row_inv[:, r, :], row_sum[:, r, :]).then_inc(row_inv_ready, 1)
                dve.wait_ge(row_inv_ready, r + 1)
                s0, n = self_slots(r)[0], len(self_slots(r))
                for t in range(TILES):
                    pr = probs[:, s0:s0 + n, t * P:t * P + (t + 1) * P]
                    i = nc.vector.tensor_scalar(pr, pr, row_inv[:, r, t:t + 1], None, ALU.mult)
                i.then_inc(probs_ready, 1)

            dve.wait_ge(bias_in, 16)
            for r in range(SOFTMAXES):
                s0, n = self_slots(r)[0], len(self_slots(r))
                for s, head in zip(self_slots(r), self_softmax_heads(r)):
                    b = take(f"score{s}")
                    nc.vector.scalar_tensor_tensor(probs[:, s, 0:P], b[:, 0:P], HEAD_DIM ** -0.5,
                                                   bias[:, head, P:S], ALU.mult, ALU.add)
                    took(nc.vector.scalar_tensor_tensor(probs[:, s, P:3 * P], b[:, P:3 * P], HEAD_DIM ** -0.5,
                                                        bias[:, head, :], ALU.mult, ALU.add))
                dve.wait_ge(taken["dve"], taken_count(f"score{s}"))
                for t in range(TILES):
                    i = nc.vector.tensor_reduce(row_max[:, r, t:t + 1], probs[:, s0:s0 + n, t * P:t * P + (t + 1) * P],
                                                AX.XY, ALU.max)
                i.then_inc(row_max_ready, 1)
                dve.wait_ge(row_max_ready, r + 1)
                nc.vector.tensor_scalar(neg_max[:, r, :], row_max[:, r, :], -1.0, None, ALU.mult
                                        ).then_inc(neg_max_ready, 1)
                if r >= 2:
                    self_inverse(r - 2)
            self_inverse(SOFTMAXES - 2)
            self_inverse(SOFTMAXES - 1)
            for r in range(SOFTMAXES + 1):
                if r < SOFTMAXES:
                    for s in self_slots(r):
                        if TAKER[f"probs_t{s}"] == "dve":
                            b = take(f"probs_t{s}")
                            took(nc.vector.tensor_copy(probsT[:, s % 8, :], b[:, 0:384]))
                if r >= 1 and TAKER[f"self_o{r - 1}"] == "dve":
                    b = take(f"self_o{r - 1}")
                    took(copy_self_o(nc.vector.tensor_copy, r - 1, b, oT))
            dve.wait_ge(gates_ready, 8)
            for c in range(CHUNKS):
                b = take(f"branch{c}")
                nc.vector.tensor_tensor(tmpA[:, c % 2, :], gates[:, c, :], b[:, 0:S], ALU.mult)
                took(nc.vector.tensor_tensor(tmpB[:, c % 2, :], gates[:, CHUNKS + c, :], b[:, S:2 * S], ALU.mult))
                dve.wait_ge(taken["dve"], taken_count(f"branch{c}"))
                nc.vector.tensor_tensor(hT[:, c, :], tmpA[:, c % 2, :], tmpB[:, c % 2, :], ALU.add
                                        ).then_inc(merged_ready, 1)
            for j in range(4):
                b = take(f"out{j}")
                xs = x[:, :, j * S:(j + 1) * S]
                i = nc.vector.tensor_tensor(xs, xs, b.rearrange("p (t c) -> p t c", t=TILES), ALU.add)
                took(i)
                dve.wait_ge(taken["dve"], taken_count(f"out{j}"))
                nc.vector.tensor_copy(tmpA[:, 0, 0:1], tmpA[:, 0, 0:1]).then_inc(x_ready, 1)
            normalise("cross", x, cross_xn)
            turned("cross", hT, 2 * CHUNKS)
            b = take("qcross1")
            took(nc.vector.tensor_copy(qcT[:, 2:4, :].rearrange("p a b -> p (a b)"), b))
            for h in range(CROSS_HEADS):
                b = take(f"cross_score{h}")
                nc.vector.tensor_reduce(c_max[:, h, :], b.rearrange("p (t m) -> p t m", t=TILES), AX.X, ALU.max
                                        ).then_inc(c_max_ready, 1)
                dve.wait_ge(c_max_ready, h + 1)
                nc.vector.tensor_scalar(c_neg[:, h, :], c_max[:, h, :], -(CROSS_DIM ** -0.5), None, ALU.mult
                                        ).then_inc(c_neg_ready, 1)
            for h in range(CROSS_HEADS):
                dve.wait_ge(taken["act"], taken_count(f"cross_score{h}"))
                nc.vector.reciprocal(c_inv[:, h, :], c_sum[:, h, :]).then_inc(c_inv_ready, 1)
                dve.wait_ge(c_inv_ready, h + 1)
                for t in range(TILES):
                    pr = c_probs[:, h, t * S:(t + 1) * S]
                    i = nc.vector.tensor_scalar(pr, pr, c_inv[:, h, t:t + 1], None, ALU.mult)
                i.then_inc(c_probs_ready, 1)
                if h >= 1:
                    b = take(f"cross_probs_t{h - 1}")
                    if h >= 3:
                        dve.wait_ge(product_ready, PLACE[f"cross_o{h - 3}"] + 1)
                    took(nc.vector.tensor_copy(c_probsT[:, (h - 1) % 2, :], b))
            b = take(f"cross_probs_t{CROSS_HEADS - 1}")
            dve.wait_ge(product_ready, PLACE[f"cross_o{CROSS_HEADS - 3}"] + 1)
            took(nc.vector.tensor_copy(c_probsT[:, (CROSS_HEADS - 1) % 2, :], b))
            for j in range(2):
                for t in range(TILES):
                    b = take(f"ocross{j}_{t}")
                    xs = x[:, t, j * 512:(j + 1) * 512]
                    took(nc.vector.tensor_tensor(xs, xs, b, ALU.add))
                    dve.wait_ge(taken["dve"], taken_count(f"ocross{j}_{t}"))
                    nc.vector.tensor_copy(tmpA[:, 0, 0:1], tmpA[:, 0, 0:1]).then_inc(x_ready, 1)
            normalise("ffn", x, ffn_xn)
            turned("ffn", hT, 3 * CHUNKS)
            dve.wait_ge(rows_in, 32)
            dve.wait_ge(xn_ready, 4)
            for t in range(TILES):
                i = nc.vector.tensor_tensor(h_rows[:, t, :], ffn_xn[:, t, :], g_ffn_row, ALU.mult)
            i.then_inc(h_rows_ready, 1)
            dve.wait_ge(h_rows_ready, 1)

            STEPS = 14

            def route(u, first_head_scores=None):
                base = u * STEPS
                k = [0]

                def step(instruction):
                    k[0] += 1
                    instruction.then_inc(route_step, 1)
                    wait_apart(dve, route_step, base + k[0])

                if first_head_scores is not None:
                    dve.wait_ge(taken["act"], first_head_scores)
                step(nc.vector.tensor_copy(key_cur[:].rearrange("p a b -> p (a b)"),
                                           scores[:, bass.ds(u * 2 * PEER_KEYS, 2 * PEER_KEYS)]))
                nc.vector.max(ranked[:, 0, 0, 0:8], key_cur[:, 0, :])
                step(nc.vector.max(ranked[:, 0, 1, 0:8], key_cur[:, 1, :]))
                nc.vector.match_replace(key_rest[:, 0, :], ranked[:, 0, 0, 0:8], key_cur[:, 0, :], -3e38)
                step(nc.vector.match_replace(key_rest[:, 1, :], ranked[:, 0, 1, 0:8], key_cur[:, 1, :], -3e38))
                nc.vector.max(ranked[:, 0, 0, 8:16], key_rest[:, 0, :])
                step(nc.vector.max(ranked[:, 0, 1, 8:16], key_rest[:, 1, :]))
                nc.vector.max_index(ranked_i[:, 0, 0:8], ranked[:, 0, 0, 0:8], key_cur[:, 0, :])
                nc.vector.max_index(ranked_i[:, 1, 0:8], ranked[:, 0, 1, 0:8], key_cur[:, 1, :])
                nc.vector.max_index(ranked_i[:, 0, 8:16], ranked[:, 0, 0, 8:16], key_rest[:, 0, :])
                step(nc.vector.max_index(ranked_i[:, 1, 8:16], ranked[:, 0, 1, 8:16], key_rest[:, 1, :]))
                nc.vector.tensor_scalar(ranked[:, 1, 0, :], ranked_i[:, 0, :], float(PEER_KEYS), None, ALU.mult)
                step(nc.vector.tensor_copy(ranked[:, 1, 1, :], ranked_i[:, 1, :]))
                at = 0
                for row, rows, width in PAIR_ROWS:
                    o = pairs[:, :, at:at + rows * width].rearrange("p a (r w) -> p a r w", w=width)
                    first = ranked[:, :, 0, row:row + rows].unsqueeze(3).to_broadcast([P, 2, rows, width])
                    second = ranked[:, :, 1, 0:width].unsqueeze(2).to_broadcast([P, 2, rows, width])
                    i = nc.vector.tensor_tensor(o, first, second, ALU.add)
                    at += rows * width
                step(i)
                step(nc.vector.max(top[:, 0:8], pairs[:, 0, :]))
                step(nc.vector.match_replace(pairs_rest[:], top[:, 0:8], pairs[:, 0, :], -3e38))
                nc.vector.max(top[:, 8:16], pairs_rest[:])
                step(nc.vector.tensor_scalar(neg_top[:], top[:, 0:1], -1.0, None, ALU.mult))
                nc.vector.max_index(top_at[:, 0:8], top[:, 0:8], pairs[:, 0, :])
                nc.vector.max_index(top_at[:, 8:16], top[:, 8:16], pairs_rest[:]).then_inc(top_ready, 1)
                wait_apart(dve, top_ready, u + 1)
                step(nc.vector.tensor_copy(top_atf[:], top_at[:]))
                step(nc.vector.tensor_tensor(pick[:], top_atf[:].unsqueeze(2).to_broadcast([P, TOPK, PAIRS]),
                                             iota[:].unsqueeze(1).to_broadcast([P, TOPK, PAIRS]), ALU.is_equal))
                step(nc.vector.tensor_tensor(pick[:], pick[:],
                                             pairs[:, 1, :].unsqueeze(1).to_broadcast([P, TOPK, PAIRS]), ALU.mult))
                step(nc.vector.tensor_reduce(expert_f[:], pick[:], AX.X, ALU.add))
                flat = expert[:].rearrange("p a b -> p (a b)")
                nc.vector.tensor_copy(flat[:, bass.ds((u % 2) * TOPK, TOPK)], expert_f[:]).then_inc(experts_ready, 1)
                return k[0]

            def gate_weights(u):
                dve.wait_ge(top_exp_ready, u + 1)
                nc.vector.reciprocal(top_inv[:], top_sum[:]).then_inc(gate_step, 1)
                dve.wait_ge(gate_step, u * 2 + 1)
                nc.vector.tensor_scalar(gate[:], top_exp[:], top_inv[:, 0:1], None, ALU.mult).then_inc(gate_step, 1)
                dve.wait_ge(gate_step, u * 2 + 2)

            def weights_diag(u, g):
                dve.wait_ge(acts_ready, u * (TOPK // GROUP) + (g + 1))
                dve.wait_ge(slot_free, u * TOPK + (RING + GROUP * (g + 1) - DIAGS))
                for s in range(g * GROUP, (g + 1) * GROUP):
                    i = nc.vector.tensor_scalar(diag[:, s % DIAGS, :], ident[:], acts[:, s:s + 1],
                                                gate[:, s:s + 1], ALU.mult, ALU.mult)
                i.then_inc(diag_ready, 1)

            def use_units(u, t):
                for g in range(TOPK // GROUP):
                    for s in range(g * GROUP, (g + 1) * GROUP):
                        dve.wait_ge(slot_in[s % RING], u * (16 * TOPK // RING) + 16 * (s // RING + 1))
                        row = ring[:, s % RING, 0:D]
                        i = nc.vector.tensor_tensor_reduce(row, row, h_rows[:, t, :], 1.0, 0.0, ALU.mult, ALU.add,
                                                           dots[:, s:s + 1])
                        if s % GROUP == GROUP - 1:
                            i.then_inc(dots_ready, 1)
                        if s % GROUP == 0 and g >= 1:
                            weights_diag(u, g - 1)
                weights_diag(u, TOPK // GROUP - 1)

            steps = route(0, taken_count("key_score0"))
            assert steps == STEPS
            for t in range(TILES):
                last = 1 if t == TILES - 1 else 0
                with dve.Fori(0, PEER_HEADS - last) as h:
                    u = h + t * PEER_HEADS
                    gate_weights(u)
                    if t == 0:
                        dve.wait_ge(taken["act"], taken_count("key_score7"))
                    route(u + 1)
                    use_units(u, t)
            gate_weights(UNITS - 1)
            use_units(UNITS - 1, TILES - 1)
            dve.wait_ge(slot_free, RING + UNITS * TOPK)
            nc.vector.tensor_copy(tmpA[:, 0, 0:1], tmpA[:, 0, 0:1]).then_inc(y_ready, 1)
            inverse_roots("final")
            for t in range(TILES):
                nc.vector.scalar_tensor_tensor(x[:, t, :], y[:, t, :], rstd[:, NORM["final"], t:t + 1], g_final_row,
                                               ALU.mult, ALU.mult).then_inc(final_ready, 1)

        @block.gpsimd
        def _(pool):
            for j in range(8):
                pool.wait_ge(taken["act"], taken_count(f"gate{j}"))
                g = gates[:, 2 * j:2 * j + 2, :]
                nc.gpsimd.tensor_scalar(g, g, 0.5, 0.5, ALU.mult, ALU.add).then_inc(gates_ready, 1)

            def gather(u, parity):
                pool.wait_ge(experts_ready, u + 1)
                for s in range(TOPK):
                    wait_apart(pool, slot_free, u * TOPK + (s + 1))
                    nc.gpsimd.indirect_dma_start(
                        out=ring[:, s % RING, :], out_offset=None, in_=experts,
                        in_offset=bass.IndirectOffsetOnAxis(ap=expert[:, parity, s:s + 1], axis=0),
                    ).then_inc(slot_in[s % RING], 16)

            with pool.Fori(0, UNITS, 2) as u:
                gather(u, 0)
                gather(u + 1, 1)


VALUE_PANELS = {2, 5, 8, 13, 14}


def copy_kv(copy, j, b, ckT, cV):
    if j < 2:
        return copy(ckT[:, 2 * j:2 * j + 2, :].rearrange("p a b -> p (a b)"), b)
    return copy(cV[:, :, (j - 2) * S:(j - 1) * S], b.rearrange("p (t c) -> p t c", t=TILES))


def copy_qkv(copy, j, b, qT, kT, vv):
    if j < 9:
        kind, four = j % 3, j // 3
    else:
        kind, four = (j - 9) // 2, 3 + (j - 9) % 2
    if kind == 2:
        return copy(vv[:, :, four * S:(four + 1) * S], b.rearrange("p (t c) -> p t c", t=TILES))
    dst = (qT, kT)[kind]
    return copy(dst[:, 2 * four:2 * four + 2, :].rearrange("p a b -> p (a b)"), b)


def copy_self_o(copy, r, b, oT):
    lo = HEAD_DIM * (r % 2)
    return copy(oT[lo:lo + HEAD_DIM, r // 2, :], b[lo:lo + HEAD_DIM, 0:S])


def distance_buckets():
    n = np.arange(S)
    nf = np.maximum(n, 1).astype(np.float32)
    large = 16 + (np.log(nf / np.float32(16)) / np.float32(np.log(128.0)) * np.float32(16)).astype(np.int32)
    return np.where(n < 16, n, np.minimum(large, 31))


def shape_constants():
    bucket = distance_buckets()
    onehot = np.zeros((32, LINE_PAD), np.float32)
    mask = np.full((SELF_HEADS, LINE_PAD), MASKED, np.float32)
    for at in range(LINE):
        dist = S - 1 - at
        if dist < 0:
            continue
        onehot[bucket[dist], at] = 1.0
        for head in range(SELF_HEADS):
            group = head // DIL_HEADS
            seen = (dist <= 128, dist % 4 == 0, dist % 16 == 0)[group] if group < DIL_GROUPS else True
            if seen:
                mask[head, at] = 0.0
    iota = np.broadcast_to(np.arange(PAIRS, dtype=np.float32), (P, PAIRS)).copy()
    return np.eye(P, dtype=np.float32), onehot, mask, iota


def column_panels(w, width=256):
    k, n = w.shape
    return w.reshape(k // P, P, n // width, width).transpose(2, 1, 0, 3).reshape(n // width, P, k // P * width)


def kernel(**inputs):
    import concourse.bacc as bacc
    from concourse.bass_utils import run_bass_kernel_spmd

    a = {k: np.asarray(v) for k, v in inputs.items()}
    w_in = a["w_in"][0]
    panels = np.ascontiguousarray(np.concatenate([
        column_panels(a["w_kv_cross"][0]), column_panels(w_in),
        column_panels(a["w_branch_a"][0], D), column_panels(a["w_branch_b"][0], 512),
        column_panels(a["w_out"][0]), column_panels(a["w_q_cross"][0]), column_panels(a["w_o_cross"][0], 512),
        column_panels(a["w_q_peer"][0])]))
    assert panels.shape == (len(PANELS), P, PANEL)
    gain_cols = np.concatenate([a[g].reshape(-1, P).T for g in ("g_mem", "g_mix", "g_cross", "g_ffn", "b_gate")], axis=1)
    ident, onehot, mask, iota = shape_constants()
    arrays = {
        "x": a["x"], "mem": a["mem"], "rel_bias": a["rel_bias"], "panels": panels, "keys": a["peer_sub_keys"][0],
        "experts": np.concatenate([a["peer_u"][0], a["peer_v"][0]], axis=1),
        "gain_cols": np.ascontiguousarray(gain_cols),
        "gain_rows": np.stack([a["g_ffn"][0], a["g_final"]]),
        "ident": ident, "onehot": onehot, "mask": mask, "iota": iota,
    }
    arrays = {f"in_{k}": np.ascontiguousarray(v) for k, v in arrays.items()}
    nc = bacc.Bacc("TRN2", target_bir_lowering=False, num_devices=1)
    args = [nc.dram_tensor(k, v.shape, mybir.dt.from_np(v.dtype), kind="ExternalInput").ap()
            for k, v in arrays.items()]
    out = nc.dram_tensor("out", a["x"].shape, F32, kind="ExternalOutput").ap()
    build(nc, *args, out)
    got = run_bass_kernel_spmd(nc, [arrays], core_ids=[0])
    return got.results[0]["out"]
```

```python
from contextlib import ExitStack

import numpy as np

import concourse.bass as bass
from concourse import mybir

ALU = mybir.AluOpType
ACT = mybir.ActivationFunctionType
AX = mybir.AxisListType
F32 = mybir.dt.float32
F32R = mybir.dt.float32r
U32 = mybir.dt.uint32

P = 128
D = 1024
S = 256
TILES = S // P
CHUNKS = D // P
HEAD_DIM = 64
DIL_HEADS, DIL_GROUPS = 4, 3
MOBA_HEADS = 8
SELF_HEADS = DIL_HEADS * DIL_GROUPS + MOBA_HEADS
SOFTMAXES = DIL_HEADS + MOBA_HEADS
CROSS_HEADS, CROSS_DIM = 4, 128
PEER_HEADS, PEER_KEYS, TOPK = 8, 128, 16
EPS = 1e-6
MASKED = -1e30
LINE = 383
LINE_PAD = 384

PAIR_ROWS = [(0, 1, 16), (1, 1, 8), (2, 1, 5), (3, 1, 4), (4, 1, 3), (5, 3, 2), (8, 8, 1)]
PAIRS = sum(n * w for _, n, w in PAIR_ROWS)

PANEL = 2048
PANELS = ([f"qkv{j}" for j in range(15)] + [f"gate{j}" for j in range(8)]
          + ["branch_a", "branch_b0", "branch_b1", "kv0", "kv1"] + [f"out{j}" for j in range(4)] + ["kv2", "kv3"]
          + [f"qcross{j}" for j in range(2)] + [f"ocross{j}" for j in range(2)]
          + [f"qpeer{j}" for j in range(PEER_HEADS)])
RAW_RING = 2
SPLIT_RING = 3
RING = 8
GROUP = 2
DIAGS = 4
FIRST_UNIT = [[], [], [], [0], [1], [2], [3], [4], [5, 6, 7]]
FIRST_SOFTMAX = 1
BANKS = 4


def self_softmax_heads(r):
    if r < DIL_HEADS:
        return [g * DIL_HEADS + r for g in range(DIL_GROUPS)]
    return [DIL_HEADS * DIL_GROUPS + r - DIL_HEADS]


def self_slots(r):
    if r < DIL_HEADS:
        return [r * DIL_GROUPS + g for g in range(DIL_GROUPS)]
    return [DIL_HEADS * DIL_GROUPS + r - DIL_HEADS]


def product_order():
    order = []

    def add(name, engine):
        order.append((name, engine))

    for c in range(4):
        add(f"turn_mix{c}", "both")
    add("line", "dve")
    add("keys", "act")
    for j in range(15):
        add(f"qkv{j}", "act")
    for r in range(SOFTMAXES):
        for s in self_slots(r):
            add(f"score{s}", "dve")
    for j in range(8):
        add(f"gate{j}", "act")
    for r in range(SOFTMAXES + 1):
        if r < SOFTMAXES:
            for s in self_slots(r):
                add(f"probs_t{s}", ("act", "dve")[s % 2])
        if r >= 1:
            add(f"self_o{r - 1}", "both")
    for branch in "AB":
        for c in range(4):
            add(f"branch{branch}{c}", "dve")
    for c in range(4):
        add(f"turn_mem{c}", "both")
    add("kv0", "act")
    add("kv1", "act")
    for j in range(4):
        add(f"out{j}", "dve")
    add("kv2", "act")
    add("kv3", "act")
    for c in range(4):
        add(f"turn_cross{c}", "both")
    for j in range(2):
        add(f"qcross{j}", "act")
    for h in range(CROSS_HEADS):
        add(f"cross_score{h}", "act")
    for h in range(CROSS_HEADS + 1):
        if h < CROSS_HEADS:
            add(f"cross_probs_t{h}", "dve")
        if h >= 1:
            add(f"cross_o{h - 1}", "both")
    for j in range(2):
        for t in range(TILES):
            add(f"ocross{j}_{t}", "dve")
    for c in range(4):
        add(f"turn_ffn{c}", "both")
    for h in range(PEER_HEADS + 1):
        if h < PEER_HEADS:
            add(f"qpeer{h}", "act")
        if h >= 1:
            add(f"key_score{h - 1}", "act")
    return order


PRODUCTS = product_order()
PLACE = {name: n for n, (name, _) in enumerate(PRODUCTS)}
TAKER = {name: "dve" if e == "both" else e for name, e in PRODUCTS}


def taken_count(name):
    return sum(1 for other, _ in PRODUCTS[:PLACE[name] + 1] if TAKER[other] == TAKER[name])


def high_count(name):
    return sum(1 for _, e in PRODUCTS[:PLACE[name] + 1] if e == "both")


def last_product_of_panel(panel):
    return {"branch_a": "branchA3", "branch_b0": "branchB1", "branch_b1": "branchB3",
            "ocross0": "ocross0_1", "ocross1": "ocross1_1"}.get(panel, panel)


def build(nc, x_in, mem_in, rel_bias, panels, keys_in, experts, gain_cols, gain_rows, ident_in,
          onehot_in, mask_in, iota_in, out):
    with ExitStack() as ctx:
        def sb(name, shape, dt=F32):
            return ctx.enter_context(nc.sbuf_tensor(name, shape, dt))

        def sem(name):
            return ctx.enter_context(nc.semaphore(name))

        line_dram = nc.dram_tensor("line_scratch", [P, SELF_HEADS, LINE_PAD], F32)

        x = sb("x", [P, TILES, D])
        raw = sb("raw", [P, RAW_RING, PANEL])
        w_hi = sb("w_hi", [P, SPLIT_RING, PANEL], F32R)
        w_lo = sb("w_lo", [P, SPLIT_RING, PANEL], F32R)
        h_hi = sb("h_hi", [P, CHUNKS, S], F32R)
        h_lo = sb("h_lo", [P, CHUNKS, S], F32R)
        o_hi = sb("o_hi", [P, CHUNKS, S], F32R)
        o_lo = sb("o_lo", [P, CHUNKS, S], F32R)
        ident = sb("ident", [P, P])
        gains = sb("gains", [P, 48])
        half_b = sb("half_b", [P, 16])
        iota = sb("iota", [P, PAIRS])
        keysT = sb("keysT", [P, 2, PEER_KEYS])
        qpT = sb("qpT", [P, 2, 2, S])
        work = sb("work", [P, TOPK * PAIRS])
        neg_max = sb("neg_max", [P, SOFTMAXES, TILES])
        row_max = sb("row_max", [P, SOFTMAXES, TILES])
        row_sum = sb("row_sum", [P, SOFTMAXES, TILES])
        row_inv = sb("row_inv", [P, SOFTMAXES, TILES])
        c_max = sb("c_max", [P, CROSS_HEADS, TILES])
        c_neg = sb("c_neg", [P, CROSS_HEADS, TILES])
        c_sum = sb("c_sum", [P, CROSS_HEADS, TILES])
        c_inv = sb("c_inv", [P, CROSS_HEADS, TILES])
        sumsq = sb("sumsq", [P, 5, TILES])
        meansq = sb("meansq", [P, 5, TILES])
        root = sb("root", [P, 5, TILES])
        rstd = sb("rstd", [P, 5, TILES])
        key_cur = sb("key_cur", [P, 2, PEER_KEYS])
        key_rest = sb("key_rest", [P, 2, PEER_KEYS])
        ranked = sb("ranked", [P, 2, 2, TOPK])
        ranked_i = sb("ranked_i", [P, 2, TOPK], U32)
        pairs = sb("pairs", [P, 2, PAIRS])
        pairs_rest = sb("pairs_rest", [P, PAIRS])
        top = sb("top", [P, TOPK])
        top_at = sb("top_at", [P, TOPK], U32)
        top_atf = sb("top_atf", [P, TOPK])
        expert_f = sb("expert_f", [P, TOPK])
        expert = sb("expert", [P, 2, TOPK], U32)
        neg_top = sb("neg_top", [P, 1])
        top_exp = sb("top_exp", [P, TOPK])
        top_sum = sb("top_sum", [P, 1])
        top_inv = sb("top_inv", [P, 1])
        gate = sb("gate", [P, TOPK])
        dots = sb("dots", [P, TOPK])
        acts = sb("acts", [P, TOPK])
        diag = sb("diag", [P, DIAGS, P])

        arena = sb("arena", [P, 22528])

        def part(at, *shape):
            n = int(np.prod(shape))
            flat = arena[:, at:at + n]
            if len(shape) == 1:
                return flat
            names = "abc"[:len(shape)]
            return flat.rearrange(f"p ({' '.join(names)}) -> p {' '.join(names)}",
                                  **{k: v for k, v in zip(names, shape)})

        qT = part(0, SELF_HEADS // 2, S)
        kT = part(2560, SELF_HEADS // 2, S)
        vv = part(5120, TILES, SELF_HEADS * HEAD_DIM)
        bias = part(7680, SELF_HEADS, S)
        probs = part(12800, SELF_HEADS, 384)
        gates = part(0, 2 * CHUNKS, S)
        probsT = part(7680, 8, 384)
        mix_xn = part(16896, TILES, D)
        line = part(18944, LINE_PAD)
        line_mask = part(19328, LINE_PAD)
        onehot = part(19712, LINE_PAD)
        rel_sb = part(20096, SELF_HEADS)
        keys_rows = part(20160, 2, PEER_KEYS)
        mem_rows = part(20480, TILES, D)
        qcT = part(0, CROSS_HEADS, S)
        c_probs = part(1024, CROSS_HEADS, TILES * S)
        c_probsT = part(3072, 2, TILES * S)
        cross_xn = part(5120, TILES, D)
        ffn_xn = part(7168, TILES, D)
        ckT = part(9216, CROSS_HEADS, S)
        cV = part(10240, TILES, CROSS_HEADS * CROSS_DIM)
        merged = work[:, 0:3 * S].rearrange("p (n c) -> p n c", n=3)
        pick = work[:].rearrange("p (k c) -> p k c", k=TOPK)
        ring = part(0, RING, 2 * D)
        scores = arena[:, 16384:16384 + TILES * PEER_HEADS * 2 * PEER_KEYS]
        h_rows = part(20480, TILES, D)
        g_ffn_row = part(11264, D)
        g_final_row = raw[:, (len(PANELS) - 2) % RAW_RING, 0:D]

        ps = ctx.enter_context(nc.psum_tensor("ps", [P, BANKS, 512], F32))
        y = ctx.enter_context(nc.psum_tensor("y", [P, TILES, D], F32))

        small_in = sem("small_in")
        x_loaded = [sem(f"x_loaded{t}") for t in range(TILES)]
        mem_loaded = sem("mem_loaded")
        panel_in = [sem(f"panel_in{i}") for i in range(RAW_RING)]
        w_hi_ready = sem("w_hi_ready")
        w_lo_ready = sem("w_lo_ready")
        high_ready = sem("high_ready")
        line_out = sem("line_out")
        bias_in = sem("bias_in")
        rows_in = sem("rows_in")
        final_row_in = sem("final_row_in")
        product_ready = sem("product_ready")
        taken = {"act": sem("taken_act"), "dve": sem("taken_dve")}
        sumsq_ready = sem("sumsq_ready")
        meansq_ready = sem("meansq_ready")
        root_ready = sem("root_ready")
        rstd_ready = sem("rstd_ready")
        xn_ready = sem("xn_ready")
        half_b_ready = sem("half_b_ready")
        row_max_ready = sem("row_max_ready")
        neg_max_ready = sem("neg_max_ready")
        exp_ready = sem("exp_ready")
        row_inv_ready = sem("row_inv_ready")
        probs_ready = sem("probs_ready")
        gates_ready = sem("gates_ready")
        gated = sem("gated")
        merged_sum = sem("merged_sum")
        merged_hi = sem("merged_hi")
        merged_ready = sem("merged_ready")
        c_max_ready = sem("c_max_ready")
        c_neg_ready = sem("c_neg_ready")
        c_exp_ready = sem("c_exp_ready")
        c_inv_ready = sem("c_inv_ready")
        c_probs_ready = sem("c_probs_ready")
        h_rows_ready = sem("h_rows_ready")
        route_step = sem("route_step")
        top_ready = sem("top_ready")
        top_exp_ready = sem("top_exp_ready")
        gate_step = sem("gate_step")
        experts_ready = sem("experts_ready")
        slot_in = [sem(f"slot_in{i}") for i in range(RING)]
        slot_free = sem("slot_free")
        dots_ready = sem("dots_ready")
        acts_ready = sem("acts_ready")
        diag_ready = sem("diag_ready")
        final_ready = sem("final_ready")
        out_done = sem("out_done")

        def bank(name):
            return ps[:, PLACE[name] % BANKS, :]

        NORM = {"mix": 0, "mem": 1, "cross": 2, "ffn": 3, "final": 4}
        UNITS = TILES * PEER_HEADS
        SMALL = 7

        def wait_apart(eng, semaphore, value):
            eng.wait_ge(semaphore, value)
            eng.nop(nofuse=True)

        block = ctx.enter_context(nc.Block())

        @block.sync
        def _(sp):
            def load_panel(n):
                if n >= RAW_RING:
                    sp.wait_ge(w_lo_ready, n - RAW_RING + 1)
                sp.dma_start(raw[:, n % RAW_RING, :], panels[n]).then_inc(panel_in[n % RAW_RING], 16)

            for t in range(TILES):
                sp.dma_start(x[:, t, :], x_in[0, t * P:(t + 1) * P, :]).then_inc(x_loaded[t], 16)
            load_panel(0)
            sp.dma_start(ident[:], ident_in).then_inc(small_in, 16)
            sp.dma_start(gains[:], gain_cols).then_inc(small_in, 16)
            load_panel(1)
            sp.dma_start(mem_rows, mem_in.rearrange("b (t p) d -> p (b t) d", p=P)).then_inc(mem_loaded, 16)
            sp.dma_start(iota[:], iota_in).then_inc(small_in, 16)
            sp.dma_start(rel_sb[0:rel_bias.shape[0]], rel_bias).then_inc(small_in, 16)
            sp.dma_start(onehot[0:rel_bias.shape[0]], onehot_in).then_inc(small_in, 16)
            sp.dma_start(line_mask[0:SELF_HEADS], mask_in).then_inc(small_in, 16)
            sp.dma_start(keys_rows, keys_in.rearrange("p k c -> k p c")).then_inc(small_in, 16)
            for n, name in enumerate(PANELS):
                if n < RAW_RING:
                    continue
                load_panel(n)
                if name == "qkv4":
                    sp.wait_ge(taken["dve"], taken_count("line"))
                    sp.dma_start(line_dram.ap().rearrange("q h c -> h q c"),
                                 line[0:SELF_HEADS].unsqueeze(1).to_broadcast([SELF_HEADS, P, LINE_PAD])
                                 ).then_inc(line_out, 16)
                if name == "qkv7":
                    sp.wait_ge(line_out, 16)
                    sp.dma_start(bias, bass.AP(line_dram, P - 1, [[SELF_HEADS * LINE_PAD - 1, P],
                                                                  [LINE_PAD, SELF_HEADS], [1, S]])
                                 ).then_inc(bias_in, 16)
                if name == "qcross0":
                    sp.wait_ge(merged_ready, CHUNKS)
                    sp.dma_start(g_ffn_row, gain_rows[0:1].to_broadcast([P, D])).then_inc(rows_in, 16)
            sp.wait_ge(w_lo_ready, len(PANELS) - 1)
            sp.dma_start(g_final_row, gain_rows[1:2].to_broadcast([P, D])).then_inc(final_row_in, 16)
            for t in range(TILES):
                sp.wait_ge(final_ready, t + 1)
                sp.dma_start(out[0, t * P:(t + 1) * P, :], x[:, t, :]).then_inc(out_done, 16)
            sp.wait_ge(out_done, 16 * TILES)

        @block.tensor
        def _(pe):
            def begin(name):
                n = PLACE[name]
                if n >= BANKS:
                    before = PRODUCTS[n - BANKS][0]
                    pe.wait_ge(taken[TAKER[before]], taken_count(before))
                return bank(name)

            def panel(name):
                n = PANELS.index(name)
                pe.wait_ge(w_lo_ready, n + 1)
                return w_hi[:, n % SPLIT_RING, :], w_lo[:, n % SPLIT_RING, :]

            def split_product(dst, stationary, moving, first, last):
                pe.matmul(dst, stationary[0], moving[0], start=first, stop=False)
                pe.matmul(dst, stationary[0], moving[1], start=False, stop=False)
                return pe.matmul(dst, stationary[1], moving[0], start=False, stop=last)

            def cut(pair, *index):
                return tuple(part[index] for part in pair)

            def turn(stage, xn):
                pe.wait_ge(xn_ready, NORM[stage] + 1)
                for c in range(4):
                    b = begin(f"turn_{stage}{c}")
                    for k in range(2):
                        for t in range(TILES):
                            mm = pe.transpose(b[:, k * S + t * P:k * S + (t + 1) * P],
                                              xn[:, t, (2 * c + k) * P:(2 * c + k + 1) * P], ident[:])
                    mm.then_inc(product_ready, 1)

            def channels_by_tokens(name, acts_t):
                w = panel(name)
                b = begin(name)
                for blk in range(2):
                    for k in range(CHUNKS):
                        at = k * S + blk * P
                        mm = split_product(b[:, blk * S:(blk + 1) * S], cut(w, slice(None), slice(at, at + P)),
                                           cut(acts_t, slice(None), k, slice(None)), k == 0, k == CHUNKS - 1)
                mm.then_inc(product_ready, 1)

            def tokens_by_channels(name, acts_t):
                w = panel(name)
                b = begin(name)
                for t in range(TILES):
                    for k in range(CHUNKS):
                        mm = split_product(b[:, t * S:(t + 1) * S],
                                           cut(acts_t, slice(None), k, slice(t * P, (t + 1) * P)),
                                           cut(w, slice(None), slice(k * S, (k + 1) * S)), k == 0, k == CHUNKS - 1)
                mm.then_inc(product_ready, 1)

            def all_taken(name):
                for e in ("act", "dve"):
                    count = sum(1 for other, _ in PRODUCTS[:PLACE[name] + 1] if TAKER[other] == e)
                    if count:
                        pe.wait_ge(taken[e], count)

            h = (h_hi, h_lo)
            o = (o_hi, o_lo)
            pe.wait_ge(small_in, 16 * SMALL)
            turn("mix", mix_xn)
            nb = rel_bias.shape[0]
            b = begin("line")
            pe.matmul(b[0:SELF_HEADS, 0:LINE_PAD], rel_sb[0:nb], onehot[0:nb],
                      start=True, stop=True).then_inc(product_ready, 1)
            b = begin("keys")
            for p in range(2):
                mm = pe.transpose(b[:, p * P:(p + 1) * P], keys_rows[:, p, :], ident[:])
            mm.then_inc(product_ready, 1)
            all_taken("turn_mix3")
            for j in range(15):
                if j in VALUE_PANELS:
                    tokens_by_channels(f"qkv{j}", h)
                else:
                    channels_by_tokens(f"qkv{j}", h)
            all_taken("qkv14")
            for r in range(SOFTMAXES):
                for s, head in zip(self_slots(r), self_softmax_heads(r)):
                    b = begin(f"score{s}")
                    lo = HEAD_DIM * (head % 2)
                    q = qT[lo:lo + HEAD_DIM, head // 2, :]
                    k = kT[lo:lo + HEAD_DIM, head // 2, :]
                    pe.matmul(b[:, 0:P], q[:, 0:P], k[:, 0:P], start=True, stop=True)
                    pe.matmul(b[:, P:3 * P], q[:, P:S], k, start=True, stop=True).then_inc(product_ready, 1)
            for j in range(8):
                channels_by_tokens(f"gate{j}", h)
            for r in range(SOFTMAXES + 1):
                if r < SOFTMAXES:
                    pe.wait_ge(probs_ready, r + 1)
                    for s in self_slots(r):
                        b = begin(f"probs_t{s}")
                        for i in range(3):
                            mm = pe.transpose(b[:, i * P:(i + 1) * P], probs[:, s, i * P:(i + 1) * P], ident[:])
                        mm.then_inc(product_ready, 1)
                if r >= 1:
                    b = begin(f"self_o{r - 1}")
                    all_taken(f"probs_t{self_slots(r - 1)[-1]}")
                    lo = HEAD_DIM * ((r - 1) % 2)
                    heads = self_softmax_heads(r - 1)
                    for i, head in enumerate(heads):
                        pt = probsT[:, self_slots(r - 1)[i] % 8, :]
                        v = vv[:, :, head * HEAD_DIM:(head + 1) * HEAD_DIM]
                        pe.matmul(b[lo:lo + HEAD_DIM, 0:S], v[:, 0, :], pt[:, 0:S], start=(i == 0), stop=False)
                        mm = pe.matmul(b[lo:lo + HEAD_DIM, P:S], v[:, 1, :], pt[:, S:3 * P],
                                       start=False, stop=(i == len(heads) - 1))
                    mm.then_inc(product_ready, 1)
            all_taken(f"self_o{SOFTMAXES - 1}")
            for branch, first_chunk, chunks in (("A", 0, 2), ("B", 2, 4)):
                for c in range(4):
                    w = panel("branch_a" if branch == "A" else f"branch_b{c // 2}")
                    width = PANEL // chunks
                    b = begin(f"branch{branch}{c}")
                    for i in range(2):
                        col = (2 * c + i) * P % width
                        for k in range(chunks):
                            at = k * width + col
                            mm = split_product(b[:, i * S:(i + 1) * S], cut(w, slice(None), slice(at, at + P)),
                                               cut(o, slice(None), first_chunk + k, slice(None)),
                                               k == 0, k == chunks - 1)
                    mm.then_inc(product_ready, 1)
            turn("mem", mem_rows)
            all_taken("turn_mem3")
            for j in range(2):
                channels_by_tokens(f"kv{j}", o)
            pe.wait_ge(merged_ready, CHUNKS)
            for j in range(4):
                tokens_by_channels(f"out{j}", h)
            for j in range(2, 4):
                tokens_by_channels(f"kv{j}", o)
            turn("cross", cross_xn)
            all_taken("turn_cross3")
            for j in range(2):
                channels_by_tokens(f"qcross{j}", h)
            all_taken("qcross1")
            for n in range(CROSS_HEADS):
                b = begin(f"cross_score{n}")
                for t in range(TILES):
                    mm = pe.matmul(b[:, t * S:(t + 1) * S], qcT[:, n, t * P:(t + 1) * P], ckT[:, n, :],
                                   start=True, stop=True)
                mm.then_inc(product_ready, 1)
            for n in range(CROSS_HEADS + 1):
                if n < CROSS_HEADS:
                    b = begin(f"cross_probs_t{n}")
                    pe.wait_ge(c_probs_ready, n + 1)
                    for m in range(TILES):
                        for t in range(TILES):
                            mm = pe.transpose(b[:, m * S + t * P:m * S + (t + 1) * P],
                                              c_probs[:, n, t * S + m * P:t * S + (m + 1) * P], ident[:])
                    mm.then_inc(product_ready, 1)
                if n >= 1:
                    b = begin(f"cross_o{n - 1}")
                    all_taken(f"cross_probs_t{n - 1}")
                    for m in range(TILES):
                        mm = pe.matmul(b[:, 0:S], cV[:, m, (n - 1) * P:n * P],
                                       c_probsT[:, (n - 1) % 2, m * S:(m + 1) * S],
                                       start=(m == 0), stop=(m == TILES - 1))
                    mm.then_inc(product_ready, 1)
            all_taken(f"cross_o{CROSS_HEADS - 1}")
            for j in range(2):
                w = panel(f"ocross{j}")
                for t in range(TILES):
                    b = begin(f"ocross{j}_{t}")
                    for k in range(CROSS_HEADS):
                        mm = split_product(b, cut(o, slice(None), k, slice(t * P, (t + 1) * P)),
                                           cut(w, slice(None), slice(k * 512, (k + 1) * 512)),
                                           k == 0, k == CROSS_HEADS - 1)
                    mm.then_inc(product_ready, 1)
            turn("ffn", ffn_xn)
            all_taken("turn_ffn3")

            def use_group(u, t, g):
                pe.wait_ge(diag_ready, u * (TOPK // GROUP) + (g + 1))
                for s in range(g * GROUP, (g + 1) * GROUP):
                    for half in range(2):
                        at = D + half * 512
                        mm = pe.matmul(y[:, t, half * 512:(half + 1) * 512], diag[:, s % DIAGS, :],
                                       ring[:, s % RING, at:at + 512], start=False, stop=False,
                                       skip_group_check=True)
                    mm.then_inc(slot_free, 1)

            for n in range(PEER_HEADS + 1):
                if n < PEER_HEADS:
                    channels_by_tokens(f"qpeer{n}", h)
                if n == 0:
                    for t in range(TILES):
                        for half in range(2):
                            mm = pe.matmul(y[:, t, half * 512:(half + 1) * 512], ident[:],
                                           x[:, t, half * 512:(half + 1) * 512], start=True, stop=False,
                                           skip_group_check=True)
                    mm.then_inc(slot_free, RING)
                if n >= 1:
                    b = begin(f"key_score{n - 1}")
                    all_taken(f"qpeer{n - 1}")
                    for t in range(TILES):
                        for p in range(2):
                            mm = pe.matmul(b[:, (2 * t + p) * P:(2 * t + p + 1) * P],
                                           qpT[:, (n - 1) % 2, p, t * P:(t + 1) * P], keysT[:, p, :],
                                           start=True, stop=True)
                    mm.then_inc(product_ready, 1)
                for g in FIRST_UNIT[n]:
                    use_group(0, 0, g)
            with pe.Fori(1, PEER_HEADS) as u:
                for g in range(TOPK // GROUP):
                    use_group(u, 0, g)
            with pe.Fori(PEER_HEADS, UNITS) as u:
                for g in range(TOPK // GROUP):
                    use_group(u, 1, g)

        @block.scalar
        def _(act):
            split = [0]

            def pace(name):
                while split[0] <= min(PANELS.index(name) + 2, len(PANELS) - 1):
                    n = split[0]
                    act.wait_ge(panel_in[n % RAW_RING], 16 * (n // RAW_RING + 1))
                    if n >= SPLIT_RING:
                        act.wait_ge(product_ready, PLACE[last_product_of_panel(PANELS[n - SPLIT_RING])] + 1)
                    nc.scalar.copy(w_hi[:, n % SPLIT_RING, :], raw[:, n % RAW_RING, :]).then_inc(w_hi_ready, 1)
                    split[0] += 1

            def take(name):
                act.wait_ge(product_ready, PLACE[name] + 1)
                return bank(name)

            def took(instruction):
                instruction.then_inc(taken["act"], 1)

            def squares(stage, rows):
                n = NORM[stage]
                for t in range(TILES):
                    if stage == "mix":
                        act.wait_ge(x_loaded[t], 16)
                    nc.scalar.activation(y[:, t, :], rows[:, t, :], ACT.Square,
                                         accum_out=sumsq[:, n, t:t + 1]).then_inc(sumsq_ready, 1)

            def roots(stage):
                n = NORM[stage]
                act.wait_ge(meansq_ready, n + 1)
                nc.scalar.activation(root[:, n, :], meansq[:, n, :], ACT.Sqrt).then_inc(root_ready, 1)

            def turned(stage, dst, gain):
                for c in range(4):
                    b = take(f"turn_{stage}{c}")
                    for k in range(2):
                        i = nc.scalar.activation(dst[:, 2 * c + k, :], b[:, k * S:(k + 1) * S], ACT.Copy,
                                                 scale=gains[:, gain + 2 * c + k:gain + 2 * c + k + 1])
                    i.then_inc(high_ready, 1)

            squares("mix", x)
            roots("mix")
            act.wait_ge(mem_loaded, 16)
            squares("mem", mem_rows)
            roots("mem")
            act.wait_ge(small_in, 16 * SMALL)
            turned("mix", h_hi, CHUNKS)
            b = take("keys")
            took(nc.scalar.copy(keysT[:].rearrange("p a b -> p (a b)"), b[:, 0:2 * P]))
            for j in range(15):
                pace(f"qkv{j}")
                b = take(f"qkv{j}")
                took(copy_qkv(nc.scalar.copy, j, b, qT, kT, vv))
            act.wait_ge(half_b_ready, 1)
            for r in range(SOFTMAXES):
                s0, n = self_slots(r)[0], len(self_slots(r))
                act.wait_ge(neg_max_ready, r + 1)
                for t in range(TILES):
                    pr = probs[:, s0:s0 + n, t * P:t * P + (t + 1) * P]
                    i = nc.scalar.activation(pr, pr, ACT.Exp, bias=neg_max[:, r, t:t + 1],
                                             accum_out=row_sum[:, r, t:t + 1])
                i.then_inc(exp_ready, 1)
            for j in range(8):
                pace(f"gate{j}")
                b = take(f"gate{j}")
                for k in range(2):
                    i = nc.scalar.activation(gates[:, 2 * j + k, :], b[:, k * S:(k + 1) * S], ACT.Tanh,
                                             bias=half_b[:, 2 * j + k:2 * j + k + 1], scale=0.5)
                took(i)
            pace("branch_a")
            for r in range(SOFTMAXES + 1):
                if r < SOFTMAXES:
                    for s in self_slots(r):
                        if TAKER[f"probs_t{s}"] == "act":
                            b = take(f"probs_t{s}")
                            took(nc.scalar.copy(probsT[:, s % 8, :], b[:, 0:384]))
                if r >= 1:
                    b = take(f"self_o{r - 1}")
                    self_o_high(nc.scalar.copy, r - 1, b, o_hi).then_inc(high_ready, 1)
            pace("branch_b0")
            pace("branch_b1")
            for c in range(CHUNKS):
                act.wait_ge(merged_sum, c + 1)
                nc.scalar.copy(h_hi[:, c, :], merged[:, c % 3, :]).then_inc(merged_hi, 1)
            turned("mem", o_hi, 0)
            for j in range(2):
                pace(f"kv{j}")
                b = take(f"kv{j}")
                took(copy_kv(nc.scalar.copy, j, b, ckT, cV))
            for j in range(4):
                pace(f"out{j}")
            act.wait_ge(taken["dve"], taken_count("out3"))
            squares("cross", x)
            roots("cross")
            for j in range(2, 4):
                pace(f"kv{j}")
                b = take(f"kv{j}")
                took(copy_kv(nc.scalar.copy, j, b, ckT, cV))
            turned("cross", h_hi, 2 * CHUNKS)
            for j in range(2):
                pace(f"qcross{j}")
                b = take(f"qcross{j}")
                took(nc.scalar.copy(qcT[:, 2 * j:2 * j + 2, :].rearrange("p a b -> p (a b)"), b))
            for h in range(CROSS_HEADS):
                b = take(f"cross_score{h}")
                act.wait_ge(c_neg_ready, h + 1)
                for t in range(TILES):
                    i = nc.scalar.activation(c_probs[:, h, t * S:(t + 1) * S], b[:, t * S:(t + 1) * S], ACT.Exp,
                                             bias=c_neg[:, h, t:t + 1], scale=CROSS_DIM ** -0.5,
                                             accum_out=c_sum[:, h, t:t + 1])
                took(i)
            for h in range(CROSS_HEADS):
                b = take(f"cross_o{h}")
                nc.scalar.copy(o_hi[:, h, :], b[:, 0:S]).then_inc(high_ready, 1)
            for j in range(2):
                pace(f"ocross{j}")
            act.wait_ge(taken["dve"], taken_count("ocross1_1"))
            squares("ffn", x)
            roots("ffn")
            turned("ffn", h_hi, 3 * CHUNKS)

            def expert_softmax(n):
                act.wait_ge(top_ready, n)
                nc.scalar.activation(top_exp[:], top[:], ACT.Exp, bias=neg_top[:, 0:1],
                                     accum_out=top_sum[:, 0:1]).then_inc(top_exp_ready, 1)

            def gelu(u, g):
                act.wait_ge(dots_ready, u * (TOPK // GROUP) + (g + 1))
                nc.scalar.activation(acts[:, g * GROUP:(g + 1) * GROUP], dots[:, g * GROUP:(g + 1) * GROUP],
                                     ACT.Gelu).then_inc(acts_ready, 1)

            by_unit = scores.rearrange("p (t h k) -> p t h k", t=TILES, h=PEER_HEADS)
            for h in range(PEER_HEADS + 1):
                if h < PEER_HEADS:
                    pace(f"qpeer{h}")
                    b = take(f"qpeer{h}")
                    took(nc.scalar.copy(qpT[:, h % 2, :, :].rearrange("p a b -> p (a b)"), b))
                if h >= 1:
                    b = take(f"key_score{h - 1}")
                    took(nc.scalar.copy(by_unit[:, :, h - 1, :], b.rearrange("p (t k) -> p t k", t=TILES)))
                if h == FIRST_SOFTMAX:
                    expert_softmax(1)
                if h == PEER_HEADS:
                    expert_softmax(2)
                for g in FIRST_UNIT[h]:
                    gelu(0, g)
            with act.Fori(1, UNITS - 1) as u:
                expert_softmax(u + 2)
                for g in range(TOPK // GROUP):
                    gelu(u, g)

            def final_squares(t):
                nc.scalar.activation(x[:, t, :], y[:, t, :], ACT.Square,
                                     accum_out=sumsq[:, NORM["final"], t:t + 1]).then_inc(sumsq_ready, 1)
                act.wait_ge(meansq_ready, NORM["final"] + t + 1)
                nc.scalar.activation(root[:, NORM["final"], t:t + 1], meansq[:, NORM["final"], t:t + 1],
                                     ACT.Sqrt).then_inc(root_ready, 1)

            act.wait_ge(slot_free, RING + PEER_HEADS * TOPK)
            final_squares(0)
            for g in range(TOPK // GROUP):
                gelu(UNITS - 1, g)
            act.wait_ge(slot_free, RING + UNITS * TOPK)
            final_squares(1)

        @block.vector
        def _(dve):
            def take(name):
                dve.wait_ge(product_ready, PLACE[name] + 1)
                return bank(name)

            def took(instruction):
                instruction.then_inc(taken["dve"], 1)

            split = [0]

            def pace(name):
                while split[0] <= min(PANELS.index(name) + 2, len(PANELS) - 1):
                    n = split[0]
                    dve.wait_ge(w_hi_ready, n + 1)
                    nc.vector.tensor_tensor(w_lo[:, n % SPLIT_RING, :], raw[:, n % RAW_RING, :],
                                            w_hi[:, n % SPLIT_RING, :].bitcast(F32), ALU.subtract
                                            ).then_inc(w_lo_ready, 1)
                    split[0] += 1

            def inverse_roots(stage):
                n = NORM[stage]
                dve.wait_ge(sumsq_ready, TILES * (n + 1))
                nc.vector.tensor_scalar(meansq[:, n, :], sumsq[:, n, :], 1.0 / D, EPS, ALU.mult, ALU.add
                                        ).then_inc(meansq_ready, 1)
                dve.wait_ge(root_ready, n + 1)
                nc.vector.reciprocal(rstd[:, n, :], root[:, n, :]).then_inc(rstd_ready, 1)
                dve.wait_ge(rstd_ready, n + 1)

            def normalise(stage, rows, xn):
                inverse_roots(stage)
                for t in range(TILES):
                    i = nc.vector.tensor_scalar(xn[:, t, :], rows[:, t, :], rstd[:, NORM[stage], t:t + 1], None,
                                                ALU.mult)
                i.then_inc(xn_ready, 1)

            def turned(stage, hi, lo, gain):
                for c in range(4):
                    b = take(f"turn_{stage}{c}")
                    dve.wait_ge(high_ready, high_count(f"turn_{stage}{c}"))
                    for k in range(2):
                        n = 2 * c + k
                        i = nc.vector.scalar_tensor_tensor(lo[:, n, :], b[:, k * S:(k + 1) * S],
                                                           gains[:, gain + n:gain + n + 1],
                                                           hi[:, n, :].bitcast(F32), ALU.mult, ALU.subtract)
                    took(i)

            normalise("mix", x, mix_xn)
            normalise("mem", mem_rows, mem_rows)
            dve.wait_ge(small_in, 16 * SMALL)
            nc.vector.tensor_scalar(half_b[:], gains[:, 32:48], 0.5, None, ALU.mult).then_inc(half_b_ready, 1)
            turned("mix", h_hi, h_lo, CHUNKS)
            b = take("line")
            took(nc.vector.tensor_tensor(line[0:SELF_HEADS], b[0:SELF_HEADS, 0:LINE_PAD], line_mask[0:SELF_HEADS],
                                         ALU.add))
            for j in range(15):
                pace(f"qkv{j}")

            def self_inverse(r):
                dve.wait_ge(exp_ready, r + 1)
                nc.vector.reciprocal(row_inv[:, r, :], row_sum[:, r, :]).then_inc(row_inv_ready, 1)
                dve.wait_ge(row_inv_ready, r + 1)
                s0, n = self_slots(r)[0], len(self_slots(r))
                for t in range(TILES):
                    pr = probs[:, s0:s0 + n, t * P:t * P + (t + 1) * P]
                    i = nc.vector.tensor_scalar(pr, pr, row_inv[:, r, t:t + 1], None, ALU.mult)
                i.then_inc(probs_ready, 1)

            dve.wait_ge(bias_in, 16)
            for r in range(SOFTMAXES):
                s0, n = self_slots(r)[0], len(self_slots(r))
                for s, head in zip(self_slots(r), self_softmax_heads(r)):
                    b = take(f"score{s}")
                    nc.vector.scalar_tensor_tensor(probs[:, s, 0:P], b[:, 0:P], HEAD_DIM ** -0.5,
                                                   bias[:, head, P:S], ALU.mult, ALU.add)
                    took(nc.vector.scalar_tensor_tensor(probs[:, s, P:3 * P], b[:, P:3 * P], HEAD_DIM ** -0.5,
                                                        bias[:, head, :], ALU.mult, ALU.add))
                dve.wait_ge(taken["dve"], taken_count(f"score{s}"))
                for t in range(TILES):
                    i = nc.vector.tensor_reduce(row_max[:, r, t:t + 1], probs[:, s0:s0 + n, t * P:t * P + (t + 1) * P],
                                                AX.XY, ALU.max)
                i.then_inc(row_max_ready, 1)
                dve.wait_ge(row_max_ready, r + 1)
                nc.vector.tensor_scalar(neg_max[:, r, :], row_max[:, r, :], -1.0, None, ALU.mult
                                        ).then_inc(neg_max_ready, 1)
                if r >= 2:
                    self_inverse(r - 2)
            self_inverse(SOFTMAXES - 2)
            self_inverse(SOFTMAXES - 1)
            for j in range(8):
                pace(f"gate{j}")
            pace("branch_a")
            for r in range(SOFTMAXES + 1):
                if r < SOFTMAXES:
                    for s in self_slots(r):
                        if TAKER[f"probs_t{s}"] == "dve":
                            b = take(f"probs_t{s}")
                            took(nc.vector.tensor_copy(probsT[:, s % 8, :], b[:, 0:384]))
                if r >= 1:
                    b = take(f"self_o{r - 1}")
                    dve.wait_ge(high_ready, high_count(f"self_o{r - 1}"))
                    took(self_o_low(nc.vector.tensor_tensor, r - 1, b, o_hi, o_lo))
            dve.wait_ge(gates_ready, 8)
            for c in range(4):
                b = take(f"branchA{c}")
                g = gates[:, 2 * c:2 * c + 2, :].rearrange("p a b -> p (a b)")
                took(nc.vector.tensor_tensor(g, g, b, ALU.mult))
            pace("branch_b0")

            def merge_low(c):
                dve.wait_ge(merged_hi, c + 1)
                nc.vector.tensor_tensor(h_lo[:, c, :], merged[:, c % 3, :], h_hi[:, c, :].bitcast(F32),
                                        ALU.subtract).then_inc(merged_ready, 1)

            for c in range(4):
                b = take(f"branchB{c}")
                g = gates[:, CHUNKS + 2 * c:CHUNKS + 2 * c + 2, :].rearrange("p a b -> p (a b)")
                took(nc.vector.tensor_tensor(g, g, b, ALU.mult))
                dve.wait_ge(taken["dve"], taken_count(f"branchB{c}"))
                for n in (2 * c, 2 * c + 1):
                    nc.vector.tensor_tensor(merged[:, n % 3, :], gates[:, n, :], gates[:, CHUNKS + n, :], ALU.add
                                            ).then_inc(merged_sum, 1)
                    if n >= 1:
                        merge_low(n - 1)
                if c == 1:
                    pace("branch_b1")
            merge_low(CHUNKS - 1)
            turned("mem", o_hi, o_lo, 0)
            pace("kv0")
            pace("kv1")
            for j in range(4):
                pace(f"out{j}")
                b = take(f"out{j}")
                xs = x[:, :, j * S:(j + 1) * S]
                took(nc.vector.tensor_tensor(xs, xs, b.rearrange("p (t c) -> p t c", t=TILES), ALU.add))
            normalise("cross", x, cross_xn)
            pace("kv2")
            pace("kv3")
            turned("cross", h_hi, h_lo, 2 * CHUNKS)
            pace("qcross0")
            pace("qcross1")
            for h in range(CROSS_HEADS):
                b = take(f"cross_score{h}")
                nc.vector.tensor_reduce(c_max[:, h, :], b.rearrange("p (t m) -> p t m", t=TILES), AX.X, ALU.max
                                        ).then_inc(c_max_ready, 1)
                dve.wait_ge(c_max_ready, h + 1)
                nc.vector.tensor_scalar(c_neg[:, h, :], c_max[:, h, :], -(CROSS_DIM ** -0.5), None, ALU.mult
                                        ).then_inc(c_neg_ready, 1)
            for h in range(CROSS_HEADS + 2):
                if h < CROSS_HEADS:
                    dve.wait_ge(taken["act"], taken_count(f"cross_score{h}"))
                    nc.vector.reciprocal(c_inv[:, h, :], c_sum[:, h, :]).then_inc(c_inv_ready, 1)
                    dve.wait_ge(c_inv_ready, h + 1)
                    for t in range(TILES):
                        pr = c_probs[:, h, t * S:(t + 1) * S]
                        i = nc.vector.tensor_scalar(pr, pr, c_inv[:, h, t:t + 1], None, ALU.mult)
                    i.then_inc(c_probs_ready, 1)
                if 1 <= h <= CROSS_HEADS:
                    b = take(f"cross_probs_t{h - 1}")
                    if h >= 3:
                        dve.wait_ge(product_ready, PLACE[f"cross_o{h - 3}"] + 1)
                    took(nc.vector.tensor_copy(c_probsT[:, (h - 1) % 2, :], b))
                if h >= 2:
                    b = take(f"cross_o{h - 2}")
                    dve.wait_ge(high_ready, high_count(f"cross_o{h - 2}"))
                    took(nc.vector.tensor_tensor(o_lo[:, h - 2, :], b[:, 0:S], o_hi[:, h - 2, :].bitcast(F32),
                                                 ALU.subtract))
            for j in range(2):
                pace(f"ocross{j}")
                for t in range(TILES):
                    b = take(f"ocross{j}_{t}")
                    xs = x[:, t, j * 512:(j + 1) * 512]
                    took(nc.vector.tensor_tensor(xs, xs, b, ALU.add))
            normalise("ffn", x, ffn_xn)
            turned("ffn", h_hi, h_lo, 3 * CHUNKS)
            dve.wait_ge(rows_in, 16)
            dve.wait_ge(xn_ready, NORM["ffn"] + 1)
            for t in range(TILES):
                i = nc.vector.tensor_tensor(h_rows[:, t, :], ffn_xn[:, t, :], g_ffn_row, ALU.mult)
            i.then_inc(h_rows_ready, 1)

            STEPS = 14

            def route(u, first_head_scores=None):
                base = u * STEPS
                k = [0]

                def step(instruction):
                    k[0] += 1
                    instruction.then_inc(route_step, 1)
                    wait_apart(dve, route_step, base + k[0])

                if first_head_scores is not None:
                    dve.wait_ge(taken["act"], first_head_scores)
                step(nc.vector.tensor_copy(key_cur[:].rearrange("p a b -> p (a b)"),
                                           scores[:, bass.ds(u * 2 * PEER_KEYS, 2 * PEER_KEYS)]))
                nc.vector.max(ranked[:, 0, 0, 0:8], key_cur[:, 0, :])
                step(nc.vector.max(ranked[:, 0, 1, 0:8], key_cur[:, 1, :]))
                nc.vector.match_replace(key_rest[:, 0, :], ranked[:, 0, 0, 0:8], key_cur[:, 0, :], -3e38)
                step(nc.vector.match_replace(key_rest[:, 1, :], ranked[:, 0, 1, 0:8], key_cur[:, 1, :], -3e38))
                nc.vector.max(ranked[:, 0, 0, 8:16], key_rest[:, 0, :])
                step(nc.vector.max(ranked[:, 0, 1, 8:16], key_rest[:, 1, :]))
                nc.vector.max_index(ranked_i[:, 0, 0:8], ranked[:, 0, 0, 0:8], key_cur[:, 0, :])
                nc.vector.max_index(ranked_i[:, 1, 0:8], ranked[:, 0, 1, 0:8], key_cur[:, 1, :])
                nc.vector.max_index(ranked_i[:, 0, 8:16], ranked[:, 0, 0, 8:16], key_rest[:, 0, :])
                step(nc.vector.max_index(ranked_i[:, 1, 8:16], ranked[:, 0, 1, 8:16], key_rest[:, 1, :]))
                nc.vector.tensor_scalar(ranked[:, 1, 0, :], ranked_i[:, 0, :], float(PEER_KEYS), None, ALU.mult)
                step(nc.vector.tensor_copy(ranked[:, 1, 1, :], ranked_i[:, 1, :]))
                at = 0
                for row, rows, width in PAIR_ROWS:
                    o = pairs[:, :, at:at + rows * width].rearrange("p a (r w) -> p a r w", w=width)
                    first = ranked[:, :, 0, row:row + rows].unsqueeze(3).to_broadcast([P, 2, rows, width])
                    second = ranked[:, :, 1, 0:width].unsqueeze(2).to_broadcast([P, 2, rows, width])
                    i = nc.vector.tensor_tensor(o, first, second, ALU.add)
                    at += rows * width
                step(i)
                step(nc.vector.max(top[:, 0:8], pairs[:, 0, :]))
                step(nc.vector.match_replace(pairs_rest[:], top[:, 0:8], pairs[:, 0, :], -3e38))
                nc.vector.max(top[:, 8:16], pairs_rest[:])
                step(nc.vector.tensor_scalar(neg_top[:], top[:, 0:1], -1.0, None, ALU.mult))
                nc.vector.max_index(top_at[:, 0:8], top[:, 0:8], pairs[:, 0, :])
                nc.vector.max_index(top_at[:, 8:16], top[:, 8:16], pairs_rest[:]).then_inc(top_ready, 1)
                wait_apart(dve, top_ready, u + 1)
                step(nc.vector.tensor_copy(top_atf[:], top_at[:]))
                step(nc.vector.tensor_tensor(pick[:], top_atf[:].unsqueeze(2).to_broadcast([P, TOPK, PAIRS]),
                                             iota[:].unsqueeze(1).to_broadcast([P, TOPK, PAIRS]), ALU.is_equal))
                step(nc.vector.tensor_tensor(pick[:], pick[:],
                                             pairs[:, 1, :].unsqueeze(1).to_broadcast([P, TOPK, PAIRS]), ALU.mult))
                step(nc.vector.tensor_reduce(expert_f[:], pick[:], AX.X, ALU.add))
                flat = expert[:].rearrange("p a b -> p (a b)")
                nc.vector.tensor_copy(flat[:, bass.ds((u % 2) * TOPK, TOPK)], expert_f[:]).then_inc(experts_ready, 1)
                return k[0]

            def gate_weights(u):
                dve.wait_ge(top_exp_ready, u + 1)
                nc.vector.reciprocal(top_inv[:], top_sum[:]).then_inc(gate_step, 1)
                dve.wait_ge(gate_step, u * 2 + 1)
                nc.vector.tensor_scalar(gate[:], top_exp[:], top_inv[:, 0:1], None, ALU.mult).then_inc(gate_step, 1)
                dve.wait_ge(gate_step, u * 2 + 2)

            def weights_diag(u, g):
                dve.wait_ge(acts_ready, u * (TOPK // GROUP) + (g + 1))
                dve.wait_ge(slot_free, u * TOPK + (RING + GROUP * (g + 1) - DIAGS))
                for s in range(g * GROUP, (g + 1) * GROUP):
                    i = nc.vector.tensor_scalar(diag[:, s % DIAGS, :], ident[:], acts[:, s:s + 1],
                                                gate[:, s:s + 1], ALU.mult, ALU.mult)
                i.then_inc(diag_ready, 1)

            def dot(u, t, s):
                dve.wait_ge(slot_in[s % RING], u * (16 * TOPK // RING) + 16 * (s // RING + 1))
                row = ring[:, s % RING, 0:D]
                i = nc.vector.tensor_tensor_reduce(row, row, h_rows[:, t, :], 1.0, 0.0, ALU.mult, ALU.add,
                                                   dots[:, s:s + 1])
                if s % GROUP == GROUP - 1:
                    i.then_inc(dots_ready, 1)

            def use_unit(u, t):
                for s in range(TOPK):
                    dot(u, t, s)
                    if s % GROUP == 0 and s > 0:
                        weights_diag(u, s // GROUP - 1)
                weights_diag(u, TOPK // GROUP - 1)

            dve.wait_ge(h_rows_ready, 1)
            for h in range(PEER_HEADS + 1):
                if h < PEER_HEADS:
                    pace(f"qpeer{h}")
                if h == FIRST_SOFTMAX:
                    steps = route(0, taken_count("key_score0"))
                    assert steps == STEPS
                    gate_weights(0)
                if h == PEER_HEADS:
                    route(1, taken_count(f"key_score{PEER_HEADS - 1}"))
                for g in FIRST_UNIT[h]:
                    for s in range(g * GROUP, (g + 1) * GROUP):
                        dot(0, 0, s)
                    weights_diag(0, g)
            with dve.Fori(1, PEER_HEADS) as u:
                gate_weights(u)
                route(u + 1)
                use_unit(u, 0)
            with dve.Fori(PEER_HEADS, UNITS - 1) as u:
                gate_weights(u)
                route(u + 1)
                use_unit(u, 1)

            def finish(t):
                n = NORM["final"]
                dve.wait_ge(sumsq_ready, TILES * n + t + 1)
                nc.vector.tensor_scalar(meansq[:, n, t:t + 1], sumsq[:, n, t:t + 1], 1.0 / D, EPS, ALU.mult, ALU.add
                                        ).then_inc(meansq_ready, 1)
                dve.wait_ge(root_ready, n + t + 1)
                nc.vector.reciprocal(rstd[:, n, t:t + 1], root[:, n, t:t + 1]).then_inc(rstd_ready, 1)
                dve.wait_ge(rstd_ready, n + t + 1)
                nc.vector.scalar_tensor_tensor(x[:, t, :], y[:, t, :], rstd[:, n, t:t + 1], g_final_row,
                                               ALU.mult, ALU.mult).then_inc(final_ready, 1)

            gate_weights(UNITS - 1)
            dve.wait_ge(final_row_in, 16)
            finish(0)
            use_unit(UNITS - 1, TILES - 1)
            finish(1)

        @block.gpsimd
        def _(pool):
            for j in range(8):
                pool.wait_ge(taken["act"], taken_count(f"gate{j}"))
                g = gates[:, 2 * j:2 * j + 2, :]
                nc.gpsimd.tensor_scalar(g, g, 0.5, 0.5, ALU.mult, ALU.add).then_inc(gates_ready, 1)

            def gather(u, parity):
                pool.wait_ge(experts_ready, u + 1)
                for s in range(TOPK):
                    wait_apart(pool, slot_free, u * TOPK + (s + 1))
                    nc.gpsimd.indirect_dma_start(
                        out=ring[:, s % RING, :], out_offset=None, in_=experts,
                        in_offset=bass.IndirectOffsetOnAxis(ap=expert[:, parity, s:s + 1], axis=0),
                    ).then_inc(slot_in[s % RING], 16)

            with pool.Fori(0, UNITS, 2) as u:
                gather(u, 0)
                gather(u + 1, 1)


VALUE_PANELS = {2, 5, 8, 13, 14}


def copy_kv(copy, j, b, ckT, cV):
    if j < 2:
        return copy(ckT[:, 2 * j:2 * j + 2, :].rearrange("p a b -> p (a b)"), b)
    return copy(cV[:, :, (j - 2) * S:(j - 1) * S], b.rearrange("p (t c) -> p t c", t=TILES))


def copy_qkv(copy, j, b, qT, kT, vv):
    if j < 9:
        kind, four = j % 3, j // 3
    else:
        kind, four = (j - 9) // 2, 3 + (j - 9) % 2
    if kind == 2:
        return copy(vv[:, :, four * S:(four + 1) * S], b.rearrange("p (t c) -> p t c", t=TILES))
    dst = (qT, kT)[kind]
    return copy(dst[:, 2 * four:2 * four + 2, :].rearrange("p a b -> p (a b)"), b)


def self_o_high(copy, r, b, o_hi):
    lo = HEAD_DIM * (r % 2)
    return copy(o_hi[lo:lo + HEAD_DIM, r // 2, :], b[lo:lo + HEAD_DIM, 0:S])


def self_o_low(tensor_tensor, r, b, o_hi, o_lo):
    lo = HEAD_DIM * (r % 2)
    return tensor_tensor(o_lo[lo:lo + HEAD_DIM, r // 2, :], b[lo:lo + HEAD_DIM, 0:S],
                         o_hi[lo:lo + HEAD_DIM, r // 2, :].bitcast(F32), ALU.subtract)


def distance_buckets():
    n = np.arange(S)
    nf = np.maximum(n, 1).astype(np.float32)
    large = 16 + (np.log(nf / np.float32(16)) / np.float32(np.log(128.0)) * np.float32(16)).astype(np.int32)
    return np.where(n < 16, n, np.minimum(large, 31))


def shape_constants():
    bucket = distance_buckets()
    onehot = np.zeros((32, LINE_PAD), np.float32)
    mask = np.full((SELF_HEADS, LINE_PAD), MASKED, np.float32)
    for at in range(LINE):
        dist = S - 1 - at
        if dist < 0:
            continue
        onehot[bucket[dist], at] = 1.0
        for head in range(SELF_HEADS):
            group = head // DIL_HEADS
            seen = (dist <= 128, dist % 4 == 0, dist % 16 == 0)[group] if group < DIL_GROUPS else True
            if seen:
                mask[head, at] = 0.0
    iota = np.broadcast_to(np.arange(PAIRS, dtype=np.float32), (P, PAIRS)).copy()
    return np.eye(P, dtype=np.float32), onehot, mask, iota


def column_panels(w, width=256):
    k, n = w.shape
    return w.reshape(k // P, P, n // width, width).transpose(2, 1, 0, 3).reshape(n // width, P, k // P * width)


def kernel(**inputs):
    import concourse.bacc as bacc
    from concourse.bass_utils import run_bass_kernel_spmd

    a = {k: np.asarray(v) for k, v in inputs.items()}
    w_in = a["w_in"][0]
    kv = column_panels(a["w_kv_cross"][0])
    panels = np.ascontiguousarray(np.concatenate([
        column_panels(w_in), column_panels(a["w_branch_a"][0], D), column_panels(a["w_branch_b"][0], 512),
        kv[:2], column_panels(a["w_out"][0]), kv[2:], column_panels(a["w_q_cross"][0]),
        column_panels(a["w_o_cross"][0], 512),
        column_panels(a["w_q_peer"][0])]))
    assert panels.shape == (len(PANELS), P, PANEL)
    gain_cols = np.concatenate([a[g].reshape(-1, P).T for g in ("g_mem", "g_mix", "g_cross", "g_ffn", "b_gate")], axis=1)
    ident, onehot, mask, iota = shape_constants()
    arrays = {
        "x": a["x"], "mem": a["mem"], "rel_bias": a["rel_bias"], "panels": panels, "keys": a["peer_sub_keys"][0],
        "experts": np.concatenate([a["peer_u"][0], a["peer_v"][0]], axis=1),
        "gain_cols": np.ascontiguousarray(gain_cols),
        "gain_rows": np.stack([a["g_ffn"][0], a["g_final"]]),
        "ident": ident, "onehot": onehot, "mask": mask, "iota": iota,
    }
    arrays = {f"in_{k}": np.ascontiguousarray(v) for k, v in arrays.items()}
    nc = bacc.Bacc("TRN2", target_bir_lowering=False, num_devices=1)
    args = [nc.dram_tensor(k, v.shape, mybir.dt.from_np(v.dtype), kind="ExternalInput").ap()
            for k, v in arrays.items()]
    out = nc.dram_tensor("out", a["x"].shape, F32, kind="ExternalOutput").ap()
    build(nc, *args, out)
    got = run_bass_kernel_spmd(nc, [arrays], core_ids=[0])
    return got.results[0]["out"]
```

```python
from contextlib import ExitStack

import numpy as np

import concourse.bass as bass
from concourse import mybir

ALU = mybir.AluOpType
ACT = mybir.ActivationFunctionType
AX = mybir.AxisListType
F32 = mybir.dt.float32
F32R = mybir.dt.float32r
U32 = mybir.dt.uint32

P = 128
D = 1024
S = 256
TILES = S // P
CHUNKS = D // P
HEAD_DIM = 64
DIL_HEADS, DIL_GROUPS = 4, 3
MOBA_HEADS = 8
SELF_HEADS = DIL_HEADS * DIL_GROUPS + MOBA_HEADS
SOFTMAXES = DIL_HEADS + MOBA_HEADS
CROSS_HEADS, CROSS_DIM = 4, 128
PEER_HEADS, PEER_KEYS, TOPK = 8, 128, 16
EPS = 1e-6
MASKED = -1e30
LINE = 383
LINE_PAD = 384

PAIR_ROWS = [(0, 1, 16), (1, 1, 8), (2, 1, 5), (3, 1, 4), (4, 1, 3), (5, 3, 2), (8, 8, 1)]
PAIRS = sum(n * w for _, n, w in PAIR_ROWS)

PANEL = 2048
PANELS = ([f"qkv{j}" for j in range(15)] + [f"gate{j}" for j in range(8)]
          + ["branch_a", "branch_b0", "branch_b1", "kv0", "kv1"] + [f"out{j}" for j in range(4)] + ["kv2", "kv3"]
          + [f"qcross{j}" for j in range(2)] + [f"ocross{j}" for j in range(2)]
          + [f"qpeer{j}" for j in range(PEER_HEADS)])
POOL_PANEL = PANELS.index("qpeer3")
RAW_RING = 2
SPLIT_RING = 3
RING = 8
GROUP = 2
DIAGS = 4
FIRST_WEIGHTS = [[], [], [], [0], [], [1], [], [2], [3, 4, 5, 6, 7]]
FIRST_UNIT = [[], [], [], [], [], [0], [], [1], [2, 3, 4, 5, 6, 7]]
FIRST_SOFTMAX = 1
SECOND_ROUTE = 3
SECOND_SOFTMAX = 5
BANKS = 4


def self_softmax_heads(r):
    if r < DIL_HEADS:
        return [g * DIL_HEADS + r for g in range(DIL_GROUPS)]
    return [DIL_HEADS * DIL_GROUPS + r - DIL_HEADS]


def self_slots(r):
    if r < DIL_HEADS:
        return [r * DIL_GROUPS + g for g in range(DIL_GROUPS)]
    return [DIL_HEADS * DIL_GROUPS + r - DIL_HEADS]


GATE_AFTER_SCORES = {3: 0, 7: 1}
GATE_AFTER_TURN = {1: 2, 3: 3, 5: 4, 7: 5, 9: 6, 11: 7}


def product_order():
    order = []

    def add(name, engine):
        order.append((name, engine))

    for c in range(4):
        add(f"turn_mix{c}", "both")
    add("line", "dve")
    add("keys", "act")
    for j in range(15):
        add(f"qkv{j}", "act")
    for r in range(SOFTMAXES):
        for s in self_slots(r):
            add(f"score{s}", "dve")
        if r in GATE_AFTER_SCORES:
            add(f"gate{GATE_AFTER_SCORES[r]}", "act")
    for r in range(SOFTMAXES + 1):
        if r < SOFTMAXES:
            for s in self_slots(r):
                add(f"probs_t{s}", ("act", "dve")[s % 2])
        if r in GATE_AFTER_TURN:
            add(f"gate{GATE_AFTER_TURN[r]}", "act")
        if r >= 1:
            add(f"self_o{r - 1}", "both")
    for c in range(4):
        add(f"turn_mem{c}", "both")
    for branch in "AB":
        for c in range(4):
            add(f"branch{branch}{c}", "dve")
    add("kv0", "act")
    add("kv1", "act")
    for j in range(4):
        add(f"out{j}", "dve")
    add("kv2", "act")
    for c in range(4):
        add(f"turn_cross{c}", "both")
    add("kv3", "act")
    for j in range(2):
        add(f"qcross{j}", "act")
    for h in range(CROSS_HEADS):
        add(f"cross_score{h}", "act")
    for h in range(CROSS_HEADS + 1):
        if h < CROSS_HEADS:
            add(f"cross_probs_t{h}", "dve")
        if h >= 1:
            add(f"cross_o{h - 1}", "both")
    for t in range(TILES):
        for j in range(2):
            add(f"ocross{j}_{t}", "dve")
    for c in range(4):
        add(f"turn_ffn{c}", "both")
    for h in range(PEER_HEADS + 1):
        if h < PEER_HEADS:
            add(f"qpeer{h}", "act")
        if h != 1:
            add(f"key_score{max(h - 1, 0)}", "act")
    return order


PRODUCTS = product_order()
PLACE = {name: n for n, (name, _) in enumerate(PRODUCTS)}
TAKER = {name: "dve" if e == "both" else e for name, e in PRODUCTS}


def taken_count(name):
    return sum(1 for other, _ in PRODUCTS[:PLACE[name] + 1] if TAKER[other] == TAKER[name])


def high_count(name):
    return sum(1 for _, e in PRODUCTS[:PLACE[name] + 1] if e == "both")


def last_product_of_panel(panel):
    return {"branch_a": "branchA3", "branch_b0": "branchB1", "branch_b1": "branchB3",
            "ocross0": "ocross0_1", "ocross1": "ocross1_1"}.get(panel, panel)


def build(nc, x_in, mem_in, rel_bias, panels, keys_in, experts, gain_cols, gain_rows, ident_in,
          onehot_in, mask_in, iota_in, out):
    with ExitStack() as ctx:
        def sb(name, shape, dt=F32):
            return ctx.enter_context(nc.sbuf_tensor(name, shape, dt))

        def sem(name):
            return ctx.enter_context(nc.semaphore(name))

        line_dram = nc.dram_tensor("line_scratch", [P, SELF_HEADS, LINE_PAD], F32)

        x = sb("x", [P, TILES, D])
        raw = sb("raw", [P, RAW_RING, PANEL])
        w_hi = sb("w_hi", [P, SPLIT_RING, PANEL], F32R)
        w_lo = sb("w_lo", [P, SPLIT_RING, PANEL], F32R)
        h_hi = sb("h_hi", [P, CHUNKS, S], F32R)
        h_lo = sb("h_lo", [P, CHUNKS, S], F32R)
        o_hi = sb("o_hi", [P, CHUNKS, S], F32R)
        o_lo = sb("o_lo", [P, CHUNKS, S], F32R)
        ident = sb("ident", [P, P])
        gains = sb("gains", [P, 48])
        half_b = sb("half_b", [P, 16])
        iota = sb("iota", [P, PAIRS])
        keysT = sb("keysT", [P, 2, PEER_KEYS])
        qpT = sb("qpT", [P, 2, 2, S])
        work = sb("work", [P, TOPK * PAIRS])
        neg_max = sb("neg_max", [P, SOFTMAXES, TILES])
        row_max = sb("row_max", [P, SOFTMAXES, TILES])
        row_sum = sb("row_sum", [P, SOFTMAXES, TILES])
        row_inv = sb("row_inv", [P, SOFTMAXES, TILES])
        c_max = sb("c_max", [P, CROSS_HEADS, TILES])
        c_neg = sb("c_neg", [P, CROSS_HEADS, TILES])
        c_sum = sb("c_sum", [P, CROSS_HEADS, TILES])
        c_inv = sb("c_inv", [P, CROSS_HEADS, TILES])
        sumsq = sb("sumsq", [P, 5, TILES])
        meansq = sb("meansq", [P, 5, TILES])
        root = sb("root", [P, 5, TILES])
        rstd = sb("rstd", [P, 5, TILES])
        spare = sb("spare", [P, 1])
        key_cur = sb("key_cur", [P, 2, PEER_KEYS])
        key_rest = sb("key_rest", [P, 2, PEER_KEYS])
        ranked = sb("ranked", [P, 2, 2, TOPK])
        ranked_i = sb("ranked_i", [P, 2, TOPK], U32)
        pairs = sb("pairs", [P, 2, PAIRS])
        pairs_rest = sb("pairs_rest", [P, PAIRS])
        top = sb("top", [P, TOPK])
        top_at = sb("top_at", [P, TOPK], U32)
        top_atf = sb("top_atf", [P, TOPK])
        expert_f = sb("expert_f", [P, TOPK])
        expert = sb("expert", [P, 2, TOPK], U32)
        neg_top = sb("neg_top", [P, 1])
        top_exp = sb("top_exp", [P, TOPK])
        top_sum = sb("top_sum", [P, 1])
        top_inv = sb("top_inv", [P, 1])
        gate = sb("gate", [P, TOPK])
        dots = sb("dots", [P, TOPK])
        acts = sb("acts", [P, TOPK])
        diag = sb("diag", [P, DIAGS, P])

        arena = sb("arena", [P, 22528])

        def part(at, *shape):
            n = int(np.prod(shape))
            flat = arena[:, at:at + n]
            if len(shape) == 1:
                return flat
            names = "abc"[:len(shape)]
            return flat.rearrange(f"p ({' '.join(names)}) -> p {' '.join(names)}",
                                  **{k: v for k, v in zip(names, shape)})

        qT = part(0, SELF_HEADS // 2, S)
        kT = part(2560, SELF_HEADS // 2, S)
        vv = part(5120, TILES, SELF_HEADS * HEAD_DIM)
        bias = part(7680, SELF_HEADS, S)
        probs = part(12800, SELF_HEADS, 384)
        gates = part(0, 2 * CHUNKS, S)
        probsT = part(7680, 8, 384)
        mix_xn = part(16896, TILES, D)
        line = part(18944, LINE_PAD)
        line_mask = part(19328, LINE_PAD)
        onehot = part(19712, LINE_PAD)
        rel_sb = part(20096, SELF_HEADS)
        keys_rows = part(20160, 2, PEER_KEYS)
        mem_rows = part(20480, TILES, D)
        qcT = part(0, CROSS_HEADS, S)
        c_probs = part(1024, CROSS_HEADS, TILES * S)
        c_probsT = part(3072, 2, TILES * S)
        cross_xn = part(5120, TILES, D)
        ffn_xn = part(7168, TILES, D)
        ckT = part(9216, CROSS_HEADS, S)
        cV = part(10240, TILES, CROSS_HEADS * CROSS_DIM)
        pick = work[:].rearrange("p (k c) -> p k c", k=TOPK)
        ring = part(0, RING, 2 * D)
        scores = arena[:, 16384:16384 + TILES * PEER_HEADS * 2 * PEER_KEYS]
        h_rows = part(20480, TILES, D)
        g_ffn_row = part(11264, D)
        g_final_row = raw[:, (len(PANELS) - 2) % RAW_RING, 0:D]

        ps = ctx.enter_context(nc.psum_tensor("ps", [P, BANKS, 512], F32))
        y = ctx.enter_context(nc.psum_tensor("y", [P, TILES, D], F32))

        first_in = sem("first_in")
        small_in = sem("small_in")
        x_loaded = [sem(f"x_loaded{t}") for t in range(TILES)]
        mem_loaded = sem("mem_loaded")
        panel_in = [sem(f"panel_in{i}") for i in range(RAW_RING)]
        w_hi_ready = sem("w_hi_ready")
        w_lo_ready = sem("w_lo_ready")
        high_ready = sem("high_ready")
        line_out = sem("line_out")
        bias_in = sem("bias_in")
        rows_in = sem("rows_in")
        final_row_in = sem("final_row_in")
        product_ready = sem("product_ready")
        taken = {"act": sem("taken_act"), "dve": sem("taken_dve")}
        sumsq_ready = sem("sumsq_ready")
        meansq_ready = sem("meansq_ready")
        root_ready = sem("root_ready")
        rstd_ready = sem("rstd_ready")
        xn_ready = sem("xn_ready")
        half_b_ready = sem("half_b_ready")
        row_max_ready = sem("row_max_ready")
        neg_max_ready = sem("neg_max_ready")
        exp_ready = sem("exp_ready")
        row_inv_ready = sem("row_inv_ready")
        probs_ready = sem("probs_ready")
        gates_ready = sem("gates_ready")
        gated = sem("gated")
        merged_sum = sem("merged_sum")
        merged_hi = sem("merged_hi")
        merged_ready = sem("merged_ready")
        c_max_ready = sem("c_max_ready")
        c_neg_ready = sem("c_neg_ready")
        c_exp_ready = sem("c_exp_ready")
        c_inv_ready = sem("c_inv_ready")
        c_probs_ready = sem("c_probs_ready")
        h_rows_ready = sem("h_rows_ready")
        route_step = sem("route_step")
        top_ready = sem("top_ready")
        top_exp_ready = sem("top_exp_ready")
        gate_step = sem("gate_step")
        experts_ready = sem("experts_ready")
        slot_in = [sem(f"slot_in{i}") for i in range(RING)]
        slot_free = sem("slot_free")
        dots_ready = sem("dots_ready")
        acts_ready = sem("acts_ready")
        diag_ready = sem("diag_ready")
        final_ready = sem("final_ready")
        out_done = sem("out_done")

        def bank(name):
            return ps[:, PLACE[name] % BANKS, :]

        NORM = {"mix": 0, "mem": 1, "cross": 2, "ffn": 3, "final": 4}
        UNITS = TILES * PEER_HEADS
        SMALL = 5

        def gate_pair(j):
            if j in GATE_AFTER_SCORES.values():
                return qpT[:, j, :, :]
            return gates[:, 2 * j:2 * j + 2, :]

        def merged(c):
            return gates[:, c:c + 2, :]

        def wait_apart(eng, semaphore, value):
            eng.wait_ge(semaphore, value)
            eng.nop(nofuse=True)

        block = ctx.enter_context(nc.Block())

        @block.sync
        def _(sp):
            def load_panel(n):
                if n >= RAW_RING:
                    sp.wait_ge(w_lo_ready, n - RAW_RING + 1)
                sp.dma_start(raw[:, n % RAW_RING, :], panels[n]).then_inc(panel_in[n % RAW_RING], 16)

            for t in range(TILES):
                sp.dma_start(x[:, t, :], x_in[0, t * P:(t + 1) * P, :]).then_inc(x_loaded[t], 16)
            sp.dma_start(ident[:], ident_in).then_inc(first_in, 16)
            sp.dma_start(gains[:], gain_cols).then_inc(first_in, 16)
            load_panel(0)
            load_panel(1)
            sp.dma_start(iota[:], iota_in).then_inc(small_in, 16)
            sp.dma_start(rel_sb[0:rel_bias.shape[0]], rel_bias).then_inc(small_in, 16)
            sp.dma_start(onehot[0:rel_bias.shape[0]], onehot_in).then_inc(small_in, 16)
            sp.dma_start(line_mask[0:SELF_HEADS], mask_in).then_inc(small_in, 16)
            sp.dma_start(keys_rows, keys_in.rearrange("p k c -> k p c")).then_inc(small_in, 16)
            sp.dma_start(mem_rows, mem_in.rearrange("b (t p) d -> p (b t) d", p=P)).then_inc(mem_loaded, 16)
            for n, name in enumerate(PANELS):
                if n < RAW_RING:
                    continue
                load_panel(n)
                if name in ("qkv4", "qkv6"):
                    sp.wait_ge(taken["dve"], taken_count("line"))
                    half = SELF_HEADS // 2
                    at = half * (name == "qkv6")
                    sp.dma_start(line_dram.ap()[:, at:at + half, :].rearrange("q h c -> h q c"),
                                 line[at:at + half].unsqueeze(1).to_broadcast([half, P, LINE_PAD])
                                 ).then_inc(line_out, 16)
                if name in ("qkv8", "qkv10"):
                    sp.wait_ge(line_out, 2 * 16)
                    half = SELF_HEADS // 2
                    at = half * (name == "qkv10")
                    sp.dma_start(bias[:, at:at + half, :],
                                 bass.AP(line_dram, P - 1 + at * LINE_PAD, [[SELF_HEADS * LINE_PAD - 1, P],
                                                                            [LINE_PAD, half], [1, S]])
                                 ).then_inc(bias_in, 16)
                if name == "qcross0":
                    sp.wait_ge(merged_ready, CHUNKS // 2)
                    sp.dma_start(g_ffn_row, gain_rows[0:1].to_broadcast([P, D])).then_inc(rows_in, 16)
            sp.wait_ge(w_lo_ready, len(PANELS) - 1)
            sp.dma_start(g_final_row, gain_rows[1:2].to_broadcast([P, D])).then_inc(final_row_in, 16)
            for t in range(TILES):
                for half in range(2):
                    sp.wait_ge(final_ready, 2 * t + half + 1)
                    cols = slice(half * 512, (half + 1) * 512)
                    sp.dma_start(out[0, t * P:(t + 1) * P, cols], x[:, t, cols]).then_inc(out_done, 16)
            sp.wait_ge(out_done, 16 * 2 * TILES)

        @block.tensor
        def _(pe):
            def begin(name):
                n = PLACE[name]
                if n >= BANKS:
                    before = PRODUCTS[n - BANKS][0]
                    pe.wait_ge(taken[TAKER[before]], taken_count(before))
                return bank(name)

            def panel(name):
                n = PANELS.index(name)
                pe.wait_ge(w_lo_ready, n + 1)
                return w_hi[:, n % SPLIT_RING, :], w_lo[:, n % SPLIT_RING, :]

            def split_product(dst, stationary, moving, first, last):
                pe.matmul(dst, stationary[0], moving[0], start=first, stop=False)
                pe.matmul(dst, stationary[0], moving[1], start=False, stop=False)
                return pe.matmul(dst, stationary[1], moving[0], start=False, stop=last)

            def cut(pair, *index):
                return tuple(part[index] for part in pair)

            def turn(stage, xn):
                pe.wait_ge(xn_ready, NORM[stage] + 1)
                for c in range(4):
                    b = begin(f"turn_{stage}{c}")
                    for k in range(2):
                        for t in range(TILES):
                            mm = pe.transpose(b[:, k * S + t * P:k * S + (t + 1) * P],
                                              xn[:, t, (2 * c + k) * P:(2 * c + k + 1) * P], ident[:])
                    mm.then_inc(product_ready, 1)

            def channels_by_tokens(name, acts_t, stage=None):
                w = panel(name)
                b = begin(name)
                for blk in range(2):
                    for k in range(CHUNKS):
                        if stage and blk == 0 and k % 2 == 0:
                            all_taken(f"turn_{stage}{k // 2}")
                        at = k * S + blk * P
                        mm = split_product(b[:, blk * S:(blk + 1) * S], cut(w, slice(None), slice(at, at + P)),
                                           cut(acts_t, slice(None), k, slice(None)), k == 0, k == CHUNKS - 1)
                mm.then_inc(product_ready, 1)

            def tokens_by_channels(name, acts_t):
                w = panel(name)
                b = begin(name)
                for t in range(TILES):
                    for k in range(CHUNKS):
                        mm = split_product(b[:, t * S:(t + 1) * S],
                                           cut(acts_t, slice(None), k, slice(t * P, (t + 1) * P)),
                                           cut(w, slice(None), slice(k * S, (k + 1) * S)), k == 0, k == CHUNKS - 1)
                mm.then_inc(product_ready, 1)

            def all_taken(name):
                for e in ("act", "dve"):
                    count = sum(1 for other, _ in PRODUCTS[:PLACE[name] + 1] if TAKER[other] == e)
                    if count:
                        pe.wait_ge(taken[e], count)

            h = (h_hi, h_lo)
            o = (o_hi, o_lo)
            pe.wait_ge(first_in, 32)
            turn("mix", mix_xn)
            pe.wait_ge(small_in, 16 * SMALL)
            nb = rel_bias.shape[0]
            b = begin("line")
            pe.matmul(b[0:SELF_HEADS, 0:LINE_PAD], rel_sb[0:nb], onehot[0:nb],
                      start=True, stop=True).then_inc(product_ready, 1)
            b = begin("keys")
            for p in range(2):
                mm = pe.transpose(b[:, p * P:(p + 1) * P], keys_rows[:, p, :], ident[:])
            mm.then_inc(product_ready, 1)
            for j in range(15):
                if j in VALUE_PANELS:
                    tokens_by_channels(f"qkv{j}", h)
                else:
                    channels_by_tokens(f"qkv{j}", h, "mix" if j == 0 else None)
            all_taken("qkv14")
            for r in range(SOFTMAXES):
                for s, head in zip(self_slots(r), self_softmax_heads(r)):
                    b = begin(f"score{s}")
                    lo = HEAD_DIM * (head % 2)
                    q = qT[lo:lo + HEAD_DIM, head // 2, :]
                    k = kT[lo:lo + HEAD_DIM, head // 2, :]
                    pe.matmul(b[:, 0:P], q[:, 0:P], k[:, 0:P], start=True, stop=True)
                    pe.matmul(b[:, P:3 * P], q[:, P:S], k, start=True, stop=True).then_inc(product_ready, 1)
                if r in GATE_AFTER_SCORES:
                    channels_by_tokens(f"gate{GATE_AFTER_SCORES[r]}", h)
            for r in range(SOFTMAXES + 1):
                if r < SOFTMAXES:
                    pe.wait_ge(probs_ready, r + 1)
                    for s in self_slots(r):
                        b = begin(f"probs_t{s}")
                        for i in range(3):
                            mm = pe.transpose(b[:, i * P:(i + 1) * P], probs[:, s, i * P:(i + 1) * P], ident[:])
                        mm.then_inc(product_ready, 1)
                if r in GATE_AFTER_TURN:
                    channels_by_tokens(f"gate{GATE_AFTER_TURN[r]}", h)
                if r >= 1:
                    b = begin(f"self_o{r - 1}")
                    all_taken(f"probs_t{self_slots(r - 1)[-1]}")
                    lo = HEAD_DIM * ((r - 1) % 2)
                    heads = self_softmax_heads(r - 1)
                    for i, head in enumerate(heads):
                        pt = probsT[:, self_slots(r - 1)[i] % 8, :]
                        v = vv[:, :, head * HEAD_DIM:(head + 1) * HEAD_DIM]
                        pe.matmul(b[lo:lo + HEAD_DIM, 0:S], v[:, 0, :], pt[:, 0:S], start=(i == 0), stop=False)
                        mm = pe.matmul(b[lo:lo + HEAD_DIM, P:S], v[:, 1, :], pt[:, S:3 * P],
                                       start=False, stop=(i == len(heads) - 1))
                    mm.then_inc(product_ready, 1)
            turn("mem", mem_rows)
            all_taken(f"self_o{SOFTMAXES - 1}")
            for branch, first_chunk, chunks in (("A", 0, 2), ("B", 2, 4)):
                for c in range(4):
                    w = panel("branch_a" if branch == "A" else f"branch_b{c // 2}")
                    width = PANEL // chunks
                    b = begin(f"branch{branch}{c}")
                    for i in range(2):
                        col = (2 * c + i) * P % width
                        for k in range(chunks):
                            at = k * width + col
                            mm = split_product(b[:, i * S:(i + 1) * S], cut(w, slice(None), slice(at, at + P)),
                                               cut(o, slice(None), first_chunk + k, slice(None)),
                                               k == 0, k == chunks - 1)
                    mm.then_inc(product_ready, 1)
            all_taken("turn_mem3")
            for j in range(2):
                channels_by_tokens(f"kv{j}", h)
            pe.wait_ge(merged_ready, CHUNKS // 2)
            for j in range(4):
                tokens_by_channels(f"out{j}", o)
            tokens_by_channels("kv2", h)
            turn("cross", cross_xn)
            tokens_by_channels("kv3", h)
            all_taken("turn_cross3")
            for j in range(2):
                channels_by_tokens(f"qcross{j}", o)
            all_taken("qcross1")
            for n in range(CROSS_HEADS):
                b = begin(f"cross_score{n}")
                for t in range(TILES):
                    mm = pe.matmul(b[:, t * S:(t + 1) * S], qcT[:, n, t * P:(t + 1) * P], ckT[:, n, :],
                                   start=True, stop=True)
                mm.then_inc(product_ready, 1)
            for n in range(CROSS_HEADS + 1):
                if n < CROSS_HEADS:
                    b = begin(f"cross_probs_t{n}")
                    pe.wait_ge(c_probs_ready, n + 1)
                    for m in range(TILES):
                        for t in range(TILES):
                            mm = pe.transpose(b[:, m * S + t * P:m * S + (t + 1) * P],
                                              c_probs[:, n, t * S + m * P:t * S + (m + 1) * P], ident[:])
                    mm.then_inc(product_ready, 1)
                if n >= 1:
                    b = begin(f"cross_o{n - 1}")
                    all_taken(f"cross_probs_t{n - 1}")
                    for m in range(TILES):
                        mm = pe.matmul(b[:, 0:S], cV[:, m, (n - 1) * P:n * P],
                                       c_probsT[:, (n - 1) % 2, m * S:(m + 1) * S],
                                       start=(m == 0), stop=(m == TILES - 1))
                    mm.then_inc(product_ready, 1)
            all_taken(f"cross_o{CROSS_HEADS - 1}")
            for t in range(TILES):
                for j in range(2):
                    w = panel(f"ocross{j}")
                    b = begin(f"ocross{j}_{t}")
                    for k in range(CROSS_HEADS):
                        mm = split_product(b, cut(o, slice(None), k, slice(t * P, (t + 1) * P)),
                                           cut(w, slice(None), slice(k * 512, (k + 1) * 512)),
                                           k == 0, k == CROSS_HEADS - 1)
                    mm.then_inc(product_ready, 1)
            turn("ffn", ffn_xn)

            def use_group(u, t, g):
                pe.wait_ge(diag_ready, u * (TOPK // GROUP) + (g + 1))
                for s in range(g * GROUP, (g + 1) * GROUP):
                    for half in range(2):
                        at = D + half * 512
                        mm = pe.matmul(y[:, t, half * 512:(half + 1) * 512], diag[:, s % DIAGS, :],
                                       ring[:, s % RING, at:at + 512], start=False, stop=False,
                                       skip_group_check=True)
                    mm.then_inc(slot_free, 1)

            def start_output(t):
                for half in range(2):
                    mm = pe.matmul(y[:, t, half * 512:(half + 1) * 512], ident[:],
                                   x[:, t, half * 512:(half + 1) * 512], start=True, stop=False,
                                   skip_group_check=True)
                return mm

            for n in range(PEER_HEADS + 1):
                if n < PEER_HEADS:
                    channels_by_tokens(f"qpeer{n}", h, "ffn" if n == 0 else None)
                if n == 0:
                    start_output(0)
                if n != 1:
                    head = max(n - 1, 0)
                    b = begin(f"key_score{head}")
                    all_taken(f"qpeer{head}")
                    for t in range(TILES):
                        for p in range(2):
                            mm = pe.matmul(b[:, (2 * t + p) * P:(2 * t + p + 1) * P],
                                           qpT[:, head % 2, p, t * P:(t + 1) * P], keysT[:, p, :],
                                           start=True, stop=True)
                    mm.then_inc(product_ready, 1)
                if n == 0:
                    start_output(1).then_inc(slot_free, RING)
                for g in FIRST_UNIT[n]:
                    use_group(0, 0, g)
            with pe.Fori(1, PEER_HEADS) as u:
                for g in range(TOPK // GROUP):
                    use_group(u, 0, g)
            with pe.Fori(PEER_HEADS, UNITS) as u:
                for g in range(TOPK // GROUP):
                    use_group(u, 1, g)

        @block.scalar
        def _(act):
            split = [0]

            def split_panel(n):
                act.wait_ge(panel_in[n % RAW_RING], 16 * (n // RAW_RING + 1))
                if n >= SPLIT_RING:
                    act.wait_ge(product_ready, PLACE[last_product_of_panel(PANELS[n - SPLIT_RING])] + 1)
                nc.scalar.copy(w_hi[:, n % SPLIT_RING, :], raw[:, n % RAW_RING, :]).then_inc(w_hi_ready, 1)
                split[0] += 1

            def pace(name):
                while split[0] <= min(PANELS.index(name) + 2, len(PANELS) - 1):
                    split_panel(split[0])

            def take(name):
                act.wait_ge(product_ready, PLACE[name] + 1)
                return bank(name)

            def took(instruction):
                instruction.then_inc(taken["act"], 1)

            def squares(stage, rows):
                n = NORM[stage]
                for t in range(TILES):
                    if stage == "mix":
                        act.wait_ge(x_loaded[t], 16)
                    nc.scalar.activation(y[:, t, :], rows[:, t, :], ACT.Square,
                                         accum_out=sumsq[:, n, t:t + 1]).then_inc(sumsq_ready, 1)

            def roots(stage):
                n = NORM[stage]
                act.wait_ge(meansq_ready, n + 1)
                nc.scalar.activation(root[:, n, :], meansq[:, n, :], ACT.Sqrt).then_inc(root_ready, 1)

            def load_sqrt_table():
                nc.scalar.activation(spare[:, 0:1], row_sum[:, 0, 0:1], ACT.Sqrt)

            def turned(stage, dst, gain):
                for c in range(4):
                    b = take(f"turn_{stage}{c}")
                    for k in range(2):
                        i = nc.scalar.activation(dst[:, 2 * c + k, :], b[:, k * S:(k + 1) * S], ACT.Copy,
                                                 scale=gains[:, gain + 2 * c + k:gain + 2 * c + k + 1])
                    i.then_inc(high_ready, 1)

            squares("mix", x)
            roots("mix")
            act.wait_ge(first_in, 32)
            split_panel(0)
            turned("mix", h_hi, CHUNKS)
            b = take("keys")
            took(nc.scalar.copy(keysT[:].rearrange("p a b -> p (a b)"), b[:, 0:2 * P]))
            for j in range(15):
                pace(f"qkv{j}")
                if j == 1:
                    act.wait_ge(mem_loaded, 16)
                    squares("mem", mem_rows)
                    roots("mem")
                b = take(f"qkv{j}")
                took(copy_qkv(nc.scalar.copy, j, b, qT, kT, vv))
            act.wait_ge(half_b_ready, 1)

            def take_gate(j):
                pace(f"gate{j}")
                b = take(f"gate{j}")
                for k in range(2):
                    at = 2 * j + k
                    i = nc.scalar.activation(gate_pair(j)[:, k, :], b[:, k * S:(k + 1) * S], ACT.Tanh,
                                             bias=half_b[:, at:at + 1], scale=0.5)
                took(i)

            for r in range(SOFTMAXES):
                s0, n = self_slots(r)[0], len(self_slots(r))
                act.wait_ge(neg_max_ready, r + 1)
                for t in range(TILES):
                    pr = probs[:, s0:s0 + n, t * P:t * P + (t + 1) * P]
                    i = nc.scalar.activation(pr, pr, ACT.Exp, bias=neg_max[:, r, t:t + 1],
                                             accum_out=row_sum[:, r, t:t + 1])
                i.then_inc(exp_ready, 1)
                if r in GATE_AFTER_SCORES:
                    take_gate(GATE_AFTER_SCORES[r])
            for r in range(SOFTMAXES + 1):
                if r < SOFTMAXES:
                    for s in self_slots(r):
                        if TAKER[f"probs_t{s}"] == "act":
                            b = take(f"probs_t{s}")
                            took(nc.scalar.copy(probsT[:, s % 8, :], b[:, 0:384]))
                if r in GATE_AFTER_TURN:
                    take_gate(GATE_AFTER_TURN[r])
                if r >= 1:
                    b = take(f"self_o{r - 1}")
                    self_o_high(nc.scalar.copy, r - 1, b, o_hi).then_inc(high_ready, 1)
            turned("mem", h_hi, 0)
            pace("branch_a")
            pace("branch_b0")
            pace("branch_b1")
            act.wait_ge(product_ready, PLACE["branchB3"] + 1)
            for c in range(0, CHUNKS, 2):
                act.wait_ge(merged_sum, c // 2 + 1)
                nc.scalar.copy(o_hi[:, c:c + 2, :], merged(c)).then_inc(merged_hi, 1)
            for j in range(2):
                pace(f"kv{j}")
                b = take(f"kv{j}")
                took(copy_kv(nc.scalar.copy, j, b, ckT, cV))
            load_sqrt_table()
            for j in range(4):
                pace(f"out{j}")
            act.wait_ge(taken["dve"], taken_count("out3"))
            squares("cross", x)
            roots("cross")
            for j in range(2, 4):
                if j == 3:
                    turned("cross", o_hi, 2 * CHUNKS)
                pace(f"kv{j}")
                b = take(f"kv{j}")
                took(copy_kv(nc.scalar.copy, j, b, ckT, cV))
            for j in range(2):
                pace(f"qcross{j}")
                b = take(f"qcross{j}")
                took(nc.scalar.copy(qcT[:, 2 * j:2 * j + 2, :].rearrange("p a b -> p (a b)"), b))
            for h in range(CROSS_HEADS):
                b = take(f"cross_score{h}")
                act.wait_ge(c_neg_ready, h + 1)
                for t in range(TILES):
                    i = nc.scalar.activation(c_probs[:, h, t * S:(t + 1) * S], b[:, t * S:(t + 1) * S], ACT.Exp,
                                             bias=c_neg[:, h, t:t + 1], scale=CROSS_DIM ** -0.5,
                                             accum_out=c_sum[:, h, t:t + 1])
                took(i)
            load_sqrt_table()
            for h in range(CROSS_HEADS):
                b = take(f"cross_o{h}")
                nc.scalar.copy(o_hi[:, h, :], b[:, 0:S]).then_inc(high_ready, 1)
            pace("ocross0")
            for t in range(TILES):
                act.wait_ge(taken["dve"], taken_count(f"ocross1_{t}"))
                nc.scalar.activation(y[:, t, :], x[:, t, :], ACT.Square,
                                     accum_out=sumsq[:, NORM["ffn"], t:t + 1]).then_inc(sumsq_ready, 1)
                pace("ocross1")
            roots("ffn")
            turned("ffn", h_hi, 3 * CHUNKS)

            def expert_softmax(n):
                act.wait_ge(top_ready, n)
                nc.scalar.activation(top_exp[:], top[:], ACT.Exp, bias=neg_top[:, 0:1],
                                     accum_out=top_sum[:, 0:1]).then_inc(top_exp_ready, 1)

            def gelu(u, g):
                act.wait_ge(dots_ready, u * (TOPK // GROUP) + (g + 1))
                nc.scalar.activation(acts[:, g * GROUP:(g + 1) * GROUP], dots[:, g * GROUP:(g + 1) * GROUP],
                                     ACT.Gelu).then_inc(acts_ready, 1)

            by_unit = scores.rearrange("p (t h k) -> p t h k", t=TILES, h=PEER_HEADS)
            pace("qpeer0")
            for h in range(PEER_HEADS + 1):
                if h < PEER_HEADS:
                    b = take(f"qpeer{h}")
                    took(nc.scalar.copy(qpT[:, h % 2, :, :].rearrange("p a b -> p (a b)"), b))
                    if h > 0:
                        pace(f"qpeer{min(h + 1, PEER_HEADS - 1)}")
                if h != 1:
                    head = max(h - 1, 0)
                    b = take(f"key_score{head}")
                    took(nc.scalar.copy(by_unit[:, :, head, :], b.rearrange("p (t k) -> p t k", t=TILES)))
                if h == 0:
                    pace("qpeer1")
                if h == FIRST_SOFTMAX:
                    expert_softmax(1)
                if h == SECOND_SOFTMAX:
                    expert_softmax(2)
                for g in FIRST_WEIGHTS[h]:
                    gelu(0, g)
            with act.Fori(1, UNITS - 1) as u:
                expert_softmax(u + 2)
                for g in range(TOPK // GROUP):
                    gelu(u, g)

            def final_squares(t):
                nc.scalar.activation(x[:, t, :], y[:, t, :], ACT.Square,
                                     accum_out=sumsq[:, NORM["final"], t:t + 1]).then_inc(sumsq_ready, 1)
                act.wait_ge(meansq_ready, NORM["final"] + t + 1)
                nc.scalar.activation(root[:, NORM["final"], t:t + 1], meansq[:, NORM["final"], t:t + 1],
                                     ACT.Sqrt).then_inc(root_ready, 1)

            act.wait_ge(slot_free, RING + PEER_HEADS * TOPK)
            final_squares(0)
            for g in range(TOPK // GROUP):
                gelu(UNITS - 1, g)
            load_sqrt_table()
            act.wait_ge(slot_free, RING + UNITS * TOPK)
            final_squares(1)

        @block.vector
        def _(dve):
            def take(name):
                dve.wait_ge(product_ready, PLACE[name] + 1)
                return bank(name)

            def took(instruction):
                instruction.then_inc(taken["dve"], 1)

            split = [0]

            def split_panel(n):
                dve.wait_ge(w_hi_ready, n + 1)
                nc.vector.tensor_tensor(w_lo[:, n % SPLIT_RING, :], raw[:, n % RAW_RING, :],
                                        w_hi[:, n % SPLIT_RING, :].bitcast(F32), ALU.subtract
                                        ).then_inc(w_lo_ready, 1)
                split[0] += 1

            def pace(name):
                while split[0] <= min(PANELS.index(name) + 2, len(PANELS) - 1):
                    split_panel(split[0])

            def inverse_roots(stage):
                n = NORM[stage]
                dve.wait_ge(sumsq_ready, TILES * (n + 1))
                nc.vector.tensor_scalar(meansq[:, n, :], sumsq[:, n, :], 1.0 / D, EPS, ALU.mult, ALU.add
                                        ).then_inc(meansq_ready, 1)
                dve.wait_ge(root_ready, n + 1)
                nc.vector.reciprocal(rstd[:, n, :], root[:, n, :]).then_inc(rstd_ready, 1)
                dve.wait_ge(rstd_ready, n + 1)

            def normalise(stage, rows, xn):
                inverse_roots(stage)
                for t in range(TILES):
                    i = nc.vector.tensor_scalar(xn[:, t, :], rows[:, t, :], rstd[:, NORM[stage], t:t + 1], None,
                                                ALU.mult)
                i.then_inc(xn_ready, 1)

            def turned(stage, hi, lo, gain):
                for c in range(4):
                    b = take(f"turn_{stage}{c}")
                    dve.wait_ge(high_ready, high_count(f"turn_{stage}{c}"))
                    for k in range(2):
                        n = 2 * c + k
                        i = nc.vector.scalar_tensor_tensor(lo[:, n, :], b[:, k * S:(k + 1) * S],
                                                           gains[:, gain + n:gain + n + 1],
                                                           hi[:, n, :].bitcast(F32), ALU.mult, ALU.subtract)
                    took(i)

            normalise("mix", x, mix_xn)
            dve.wait_ge(first_in, 32)
            nc.vector.tensor_scalar(half_b[:], gains[:, 32:48], 0.5, None, ALU.mult).then_inc(half_b_ready, 1)
            split_panel(0)
            turned("mix", h_hi, h_lo, CHUNKS)
            dve.wait_ge(small_in, 16 * SMALL)
            b = take("line")
            took(nc.vector.tensor_tensor(line[0:SELF_HEADS], b[0:SELF_HEADS, 0:LINE_PAD], line_mask[0:SELF_HEADS],
                                         ALU.add))
            for j in range(15):
                pace(f"qkv{j}")
                if j == 1:
                    normalise("mem", mem_rows, mem_rows)

            def self_inverse(r):
                dve.wait_ge(exp_ready, r + 1)
                nc.vector.reciprocal(row_inv[:, r, :], row_sum[:, r, :]).then_inc(row_inv_ready, 1)

            dve.wait_ge(bias_in, 2 * 16)
            for r in range(SOFTMAXES):
                s0, n = self_slots(r)[0], len(self_slots(r))
                for s, head in zip(self_slots(r), self_softmax_heads(r)):
                    b = take(f"score{s}")
                    nc.vector.scalar_tensor_tensor(probs[:, s, 0:P], b[:, 0:P], HEAD_DIM ** -0.5,
                                                   bias[:, head, P:S], ALU.mult, ALU.add)
                    took(nc.vector.scalar_tensor_tensor(probs[:, s, P:3 * P], b[:, P:3 * P], HEAD_DIM ** -0.5,
                                                        bias[:, head, :], ALU.mult, ALU.add))
                dve.wait_ge(taken["dve"], taken_count(f"score{s}"))
                for t in range(TILES):
                    i = nc.vector.tensor_reduce(row_max[:, r, t:t + 1], probs[:, s0:s0 + n, t * P:t * P + (t + 1) * P],
                                                AX.XY, ALU.max)
                i.then_inc(row_max_ready, 1)
                dve.wait_ge(row_max_ready, r + 1)
                nc.vector.tensor_scalar(neg_max[:, r, :], row_max[:, r, :], -1.0, None, ALU.mult
                                        ).then_inc(neg_max_ready, 1)
                if r in GATE_AFTER_SCORES:
                    pace(f"gate{GATE_AFTER_SCORES[r]}")
                if r >= 2:
                    self_inverse(r - 2)
            self_inverse(SOFTMAXES - 2)
            self_inverse(SOFTMAXES - 1)
            for r in range(SOFTMAXES + 1):
                if r < SOFTMAXES:
                    for s in self_slots(r):
                        if TAKER[f"probs_t{s}"] == "dve":
                            b = take(f"probs_t{s}")
                            took(nc.vector.tensor_copy(probsT[:, s % 8, :], b[:, 0:384]))
                if r in GATE_AFTER_TURN:
                    pace(f"gate{GATE_AFTER_TURN[r]}")
                if r >= 1:
                    b = take(f"self_o{r - 1}")
                    dve.wait_ge(high_ready, high_count(f"self_o{r - 1}"))
                    took(self_o_low(nc.vector.tensor_tensor, r - 1, b, o_hi, o_lo))
            turned("mem", h_hi, h_lo, 0)
            pace("branch_a")
            dve.wait_ge(gates_ready, 8)
            for c in range(4):
                b = take(f"branchA{c}")
                g = gate_pair(c).rearrange("p a b -> p (a b)")
                took(nc.vector.tensor_tensor(merged(2 * c).rearrange("p a b -> p (a b)"), g, b, ALU.mult))
            pace("branch_b0")
            for c in range(4):
                b = take(f"branchB{c}")
                g = gates[:, CHUNKS + 2 * c:CHUNKS + 2 * c + 2, :].rearrange("p a b -> p (a b)")
                took(nc.vector.tensor_tensor(g, g, b, ALU.mult))
                if c == 1:
                    pace("branch_b1")
            pace("kv0")
            pace("kv1")
            for j in range(4):
                pace(f"out{j}")
                b = take(f"out{j}")
                xs = x[:, :, j * S:(j + 1) * S]
                took(nc.vector.tensor_tensor(xs, xs, b.rearrange("p (t c) -> p t c", t=TILES), ALU.add))
            normalise("cross", x, cross_xn)
            turned("cross", o_hi, o_lo, 2 * CHUNKS)
            pace("kv2")
            pace("kv3")
            pace("qcross0")
            pace("qcross1")
            for h in range(CROSS_HEADS):
                b = take(f"cross_score{h}")
                nc.vector.tensor_reduce(c_max[:, h, :], b.rearrange("p (t m) -> p t m", t=TILES), AX.X, ALU.max
                                        ).then_inc(c_max_ready, 1)
                dve.wait_ge(c_max_ready, h + 1)
                nc.vector.tensor_scalar(c_neg[:, h, :], c_max[:, h, :], -(CROSS_DIM ** -0.5), None, ALU.mult
                                        ).then_inc(c_neg_ready, 1)
            for h in range(CROSS_HEADS + 2):
                if h < CROSS_HEADS:
                    dve.wait_ge(taken["act"], taken_count(f"cross_score{h}"))
                    nc.vector.reciprocal(c_inv[:, h, :], c_sum[:, h, :]).then_inc(c_inv_ready, 1)
                    dve.wait_ge(c_inv_ready, h + 1)
                    for t in range(TILES):
                        pr = c_probs[:, h, t * S:(t + 1) * S]
                        i = nc.vector.tensor_scalar(pr, pr, c_inv[:, h, t:t + 1], None, ALU.mult)
                    i.then_inc(c_probs_ready, 1)
                if 1 <= h <= CROSS_HEADS:
                    b = take(f"cross_probs_t{h - 1}")
                    if h >= 3:
                        dve.wait_ge(product_ready, PLACE[f"cross_o{h - 3}"] + 1)
                    took(nc.vector.tensor_copy(c_probsT[:, (h - 1) % 2, :], b))
                if h >= 2:
                    b = take(f"cross_o{h - 2}")
                    dve.wait_ge(high_ready, high_count(f"cross_o{h - 2}"))
                    took(nc.vector.tensor_tensor(o_lo[:, h - 2, :], b[:, 0:S], o_hi[:, h - 2, :].bitcast(F32),
                                                 ALU.subtract))
            pace("ocross0")
            for t in range(TILES):
                for j in range(2):
                    b = take(f"ocross{j}_{t}")
                    xs = x[:, t, j * 512:(j + 1) * 512]
                    took(nc.vector.tensor_tensor(xs, xs, b, ALU.add))
            normalise("ffn", x, ffn_xn)
            turned("ffn", h_hi, h_lo, 3 * CHUNKS)
            pace("ocross1")
            pace("qpeer0")
            dve.wait_ge(rows_in, 16)
            dve.wait_ge(xn_ready, NORM["ffn"] + 1)
            for t in range(TILES):
                i = nc.vector.tensor_tensor(h_rows[:, t, :], ffn_xn[:, t, :], g_ffn_row, ALU.mult)
            i.then_inc(h_rows_ready, 1)

            STEPS = 14

            def route(u, first_head_scores=None):
                base = u * STEPS
                k = [0]

                def step(instruction):
                    k[0] += 1
                    instruction.then_inc(route_step, 1)
                    wait_apart(dve, route_step, base + k[0])

                if first_head_scores is not None:
                    dve.wait_ge(taken["act"], first_head_scores)
                step(nc.vector.tensor_copy(key_cur[:].rearrange("p a b -> p (a b)"),
                                           scores[:, bass.ds(u * 2 * PEER_KEYS, 2 * PEER_KEYS)]))
                nc.vector.max(ranked[:, 0, 0, 0:8], key_cur[:, 0, :])
                step(nc.vector.max(ranked[:, 0, 1, 0:8], key_cur[:, 1, :]))
                nc.vector.match_replace(key_rest[:, 0, :], ranked[:, 0, 0, 0:8], key_cur[:, 0, :], -3e38)
                step(nc.vector.match_replace(key_rest[:, 1, :], ranked[:, 0, 1, 0:8], key_cur[:, 1, :], -3e38))
                nc.vector.max(ranked[:, 0, 0, 8:16], key_rest[:, 0, :])
                step(nc.vector.max(ranked[:, 0, 1, 8:16], key_rest[:, 1, :]))
                nc.vector.max_index(ranked_i[:, 0, 0:8], ranked[:, 0, 0, 0:8], key_cur[:, 0, :])
                nc.vector.max_index(ranked_i[:, 1, 0:8], ranked[:, 0, 1, 0:8], key_cur[:, 1, :])
                nc.vector.max_index(ranked_i[:, 0, 8:16], ranked[:, 0, 0, 8:16], key_rest[:, 0, :])
                step(nc.vector.max_index(ranked_i[:, 1, 8:16], ranked[:, 0, 1, 8:16], key_rest[:, 1, :]))
                nc.vector.tensor_scalar(ranked[:, 1, 0, :], ranked_i[:, 0, :], float(PEER_KEYS), None, ALU.mult)
                step(nc.vector.tensor_copy(ranked[:, 1, 1, :], ranked_i[:, 1, :]))
                at = 0
                for row, rows, width in PAIR_ROWS:
                    o = pairs[:, :, at:at + rows * width].rearrange("p a (r w) -> p a r w", w=width)
                    first = ranked[:, :, 0, row:row + rows].unsqueeze(3).to_broadcast([P, 2, rows, width])
                    second = ranked[:, :, 1, 0:width].unsqueeze(2).to_broadcast([P, 2, rows, width])
                    i = nc.vector.tensor_tensor(o, first, second, ALU.add)
                    at += rows * width
                step(i)
                step(nc.vector.max(top[:, 0:8], pairs[:, 0, :]))
                step(nc.vector.match_replace(pairs_rest[:], top[:, 0:8], pairs[:, 0, :], -3e38))
                nc.vector.max(top[:, 8:16], pairs_rest[:])
                step(nc.vector.tensor_scalar(neg_top[:], top[:, 0:1], -1.0, None, ALU.mult))
                nc.vector.max_index(top_at[:, 0:8], top[:, 0:8], pairs[:, 0, :])
                nc.vector.max_index(top_at[:, 8:16], top[:, 8:16], pairs_rest[:]).then_inc(top_ready, 1)
                wait_apart(dve, top_ready, u + 1)
                step(nc.vector.tensor_copy(top_atf[:], top_at[:]))
                step(nc.vector.tensor_tensor(pick[:], top_atf[:].unsqueeze(2).to_broadcast([P, TOPK, PAIRS]),
                                             iota[:].unsqueeze(1).to_broadcast([P, TOPK, PAIRS]), ALU.is_equal))
                step(nc.vector.tensor_tensor(pick[:], pick[:],
                                             pairs[:, 1, :].unsqueeze(1).to_broadcast([P, TOPK, PAIRS]), ALU.mult))
                step(nc.vector.tensor_reduce(expert_f[:], pick[:], AX.X, ALU.add))
                flat = expert[:].rearrange("p a b -> p (a b)")
                nc.vector.tensor_copy(flat[:, bass.ds((u % 2) * TOPK, TOPK)], expert_f[:]).then_inc(experts_ready, 1)
                return k[0]

            def gate_weights(u):
                dve.wait_ge(top_exp_ready, u + 1)
                nc.vector.reciprocal(top_inv[:], top_sum[:]).then_inc(gate_step, 1)
                dve.wait_ge(gate_step, u * 2 + 1)
                nc.vector.tensor_scalar(gate[:], top_exp[:], top_inv[:, 0:1], None, ALU.mult).then_inc(gate_step, 1)
                dve.wait_ge(gate_step, u * 2 + 2)

            def weights_diag(u, g):
                dve.wait_ge(acts_ready, u * (TOPK // GROUP) + (g + 1))
                dve.wait_ge(slot_free, u * TOPK + (RING + GROUP * (g + 1) - DIAGS))
                for s in range(g * GROUP, (g + 1) * GROUP):
                    i = nc.vector.tensor_scalar(diag[:, s % DIAGS, :], ident[:], acts[:, s:s + 1],
                                                gate[:, s:s + 1], ALU.mult, ALU.mult)
                i.then_inc(diag_ready, 1)

            def dot(u, t, s):
                dve.wait_ge(slot_in[s % RING], u * (16 * TOPK // RING) + 16 * (s // RING + 1))
                row = ring[:, s % RING, 0:D]
                i = nc.vector.tensor_tensor_reduce(row, row, h_rows[:, t, :], 1.0, 0.0, ALU.mult, ALU.add,
                                                   dots[:, s:s + 1])
                if s % GROUP == GROUP - 1:
                    i.then_inc(dots_ready, 1)

            def use_unit(u, t):
                for s in range(TOPK):
                    dot(u, t, s)
                    if s % GROUP == 0 and s > 0:
                        weights_diag(u, s // GROUP - 1)
                weights_diag(u, TOPK // GROUP - 1)

            dve.wait_ge(h_rows_ready, 1)
            for h in range(PEER_HEADS + 1):
                if 1 < h < PEER_HEADS:
                    pace(f"qpeer{h}")
                if h == FIRST_SOFTMAX:
                    steps = route(0, taken_count("key_score0"))
                    assert steps == STEPS
                    gate_weights(0)
                    split[0] += 1
                    dve.wait_ge(w_lo_ready, POOL_PANEL + 1)
                if h == SECOND_ROUTE:
                    route(1, taken_count("key_score1"))
                for g in FIRST_WEIGHTS[h]:
                    for s in range(g * GROUP, (g + 1) * GROUP):
                        dot(0, 0, s)
                    weights_diag(0, g)
            dve.wait_ge(taken["act"], taken_count(f"key_score{PEER_HEADS - 1}"))
            with dve.Fori(1, PEER_HEADS) as u:
                gate_weights(u)
                route(u + 1)
                use_unit(u, 0)
            with dve.Fori(PEER_HEADS, UNITS - 1) as u:
                gate_weights(u)
                route(u + 1)
                use_unit(u, 1)

            def finish(t):
                n = NORM["final"]
                dve.wait_ge(sumsq_ready, TILES * n + t + 1)
                nc.vector.tensor_scalar(meansq[:, n, t:t + 1], sumsq[:, n, t:t + 1], 1.0 / D, EPS, ALU.mult, ALU.add
                                        ).then_inc(meansq_ready, 1)
                dve.wait_ge(root_ready, n + t + 1)
                nc.vector.reciprocal(rstd[:, n, t:t + 1], root[:, n, t:t + 1]).then_inc(rstd_ready, 1)
                dve.wait_ge(rstd_ready, n + t + 1)
                for half in range(2):
                    cols = slice(half * 512, (half + 1) * 512)
                    nc.vector.scalar_tensor_tensor(x[:, t, cols], y[:, t, cols], rstd[:, n, t:t + 1],
                                                   g_final_row[:, cols], ALU.mult, ALU.mult
                                                   ).then_inc(final_ready, 1)

            gate_weights(UNITS - 1)
            dve.wait_ge(final_row_in, 16)
            finish(0)
            use_unit(UNITS - 1, TILES - 1)
            finish(1)

        @block.gpsimd
        def _(pool):
            for r in range(SOFTMAXES):
                pool.wait_ge(row_inv_ready, r + 1)
                s0, n = self_slots(r)[0], len(self_slots(r))
                for t in range(TILES):
                    pr = probs[:, s0:s0 + n, t * P:t * P + (t + 1) * P]
                    i = nc.gpsimd.tensor_scalar(pr, pr, row_inv[:, r, t:t + 1], None, ALU.mult)
                i.then_inc(probs_ready, 1)
            for j in range(8):
                pool.wait_ge(taken["act"], taken_count(f"gate{j}"))
                g = gate_pair(j)
                nc.gpsimd.tensor_scalar(g, g, 0.5, 0.5, ALU.mult, ALU.add).then_inc(gates_ready, 1)
            for c in range(4):
                pool.wait_ge(taken["dve"], taken_count(f"branchB{c}"))
                m = merged(2 * c)
                nc.gpsimd.tensor_tensor(m, m, gates[:, CHUNKS + 2 * c:CHUNKS + 2 * c + 2, :], ALU.add
                                        ).then_inc(merged_sum, 1)
            for c in range(4):
                pool.wait_ge(merged_hi, c + 1)
                nc.gpsimd.tensor_tensor(o_lo[:, 2 * c:2 * c + 2, :], merged(2 * c),
                                        o_hi[:, 2 * c:2 * c + 2, :].bitcast(F32), ALU.subtract
                                        ).then_inc(merged_ready, 1)

            pool.wait_ge(w_hi_ready, POOL_PANEL + 1)
            pool.wait_ge(w_lo_ready, POOL_PANEL)
            nc.gpsimd.tensor_tensor(w_lo[:, POOL_PANEL % SPLIT_RING, :], raw[:, POOL_PANEL % RAW_RING, :],
                                    w_hi[:, POOL_PANEL % SPLIT_RING, :].bitcast(F32), ALU.subtract
                                    ).then_inc(w_lo_ready, 1)

            def gather(u, parity):
                pool.wait_ge(experts_ready, u + 1)
                for s in range(TOPK):
                    wait_apart(pool, slot_free, u * TOPK + (s + 1))
                    nc.gpsimd.indirect_dma_start(
                        out=ring[:, s % RING, :], out_offset=None, in_=experts,
                        in_offset=bass.IndirectOffsetOnAxis(ap=expert[:, parity, s:s + 1], axis=0),
                    ).then_inc(slot_in[s % RING], 16)

            with pool.Fori(0, UNITS, 2) as u:
                gather(u, 0)
                gather(u + 1, 1)


VALUE_PANELS = {2, 5, 8, 13, 14}


def copy_kv(copy, j, b, ckT, cV):
    if j < 2:
        return copy(ckT[:, 2 * j:2 * j + 2, :].rearrange("p a b -> p (a b)"), b)
    return copy(cV[:, :, (j - 2) * S:(j - 1) * S], b.rearrange("p (t c) -> p t c", t=TILES))


def copy_qkv(copy, j, b, qT, kT, vv):
    if j < 9:
        kind, four = j % 3, j // 3
    else:
        kind, four = (j - 9) // 2, 3 + (j - 9) % 2
    if kind == 2:
        return copy(vv[:, :, four * S:(four + 1) * S], b.rearrange("p (t c) -> p t c", t=TILES))
    dst = (qT, kT)[kind]
    return copy(dst[:, 2 * four:2 * four + 2, :].rearrange("p a b -> p (a b)"), b)


def self_o_high(copy, r, b, o_hi):
    lo = HEAD_DIM * (r % 2)
    return copy(o_hi[lo:lo + HEAD_DIM, r // 2, :], b[lo:lo + HEAD_DIM, 0:S])


def self_o_low(tensor_tensor, r, b, o_hi, o_lo):
    lo = HEAD_DIM * (r % 2)
    return tensor_tensor(o_lo[lo:lo + HEAD_DIM, r // 2, :], b[lo:lo + HEAD_DIM, 0:S],
                         o_hi[lo:lo + HEAD_DIM, r // 2, :].bitcast(F32), ALU.subtract)


def distance_buckets():
    n = np.arange(S)
    nf = np.maximum(n, 1).astype(np.float32)
    large = 16 + (np.log(nf / np.float32(16)) / np.float32(np.log(128.0)) * np.float32(16)).astype(np.int32)
    return np.where(n < 16, n, np.minimum(large, 31))


def shape_constants():
    bucket = distance_buckets()
    onehot = np.zeros((32, LINE_PAD), np.float32)
    mask = np.full((SELF_HEADS, LINE_PAD), MASKED, np.float32)
    for at in range(LINE):
        dist = S - 1 - at
        if dist < 0:
            continue
        onehot[bucket[dist], at] = 1.0
        for head in range(SELF_HEADS):
            group = head // DIL_HEADS
            seen = (dist <= 128, dist % 4 == 0, dist % 16 == 0)[group] if group < DIL_GROUPS else True
            if seen:
                mask[head, at] = 0.0
    iota = np.broadcast_to(np.arange(PAIRS, dtype=np.float32), (P, PAIRS)).copy()
    return np.eye(P, dtype=np.float32), onehot, mask, iota


def column_panels(w, width=256):
    k, n = w.shape
    return w.reshape(k // P, P, n // width, width).transpose(2, 1, 0, 3).reshape(n // width, P, k // P * width)


def kernel(**inputs):
    import concourse.bacc as bacc
    from concourse.bass_utils import run_bass_kernel_spmd

    a = {k: np.asarray(v) for k, v in inputs.items()}
    w_in = a["w_in"][0]
    kv = column_panels(a["w_kv_cross"][0])
    panels = np.ascontiguousarray(np.concatenate([
        column_panels(w_in), column_panels(a["w_branch_a"][0], D), column_panels(a["w_branch_b"][0], 512),
        kv[:2], column_panels(a["w_out"][0]), kv[2:], column_panels(a["w_q_cross"][0]),
        column_panels(a["w_o_cross"][0], 512),
        column_panels(a["w_q_peer"][0])]))
    assert panels.shape == (len(PANELS), P, PANEL)
    gain_cols = np.concatenate([a[g].reshape(-1, P).T for g in ("g_mem", "g_mix", "g_cross", "g_ffn", "b_gate")], axis=1)
    ident, onehot, mask, iota = shape_constants()
    arrays = {
        "x": a["x"], "mem": a["mem"], "rel_bias": a["rel_bias"], "panels": panels, "keys": a["peer_sub_keys"][0],
        "experts": np.concatenate([a["peer_u"][0], a["peer_v"][0]], axis=1),
        "gain_cols": np.ascontiguousarray(gain_cols),
        "gain_rows": np.stack([a["g_ffn"][0], a["g_final"]]),
        "ident": ident, "onehot": onehot, "mask": mask, "iota": iota,
    }
    arrays = {f"in_{k}": np.ascontiguousarray(v) for k, v in arrays.items()}
    nc = bacc.Bacc("TRN2", target_bir_lowering=False, num_devices=1)
    args = [nc.dram_tensor(k, v.shape, mybir.dt.from_np(v.dtype), kind="ExternalInput").ap()
            for k, v in arrays.items()]
    out = nc.dram_tensor("out", a["x"].shape, F32, kind="ExternalOutput").ap()
    build(nc, *args, out)
    got = run_bass_kernel_spmd(nc, [arrays], core_ids=[0])
    return got.results[0]["out"]
```
